# Optimizing a Trainium2 kernel written in Bass

```python
import jax, jax.numpy as jnp
from jax import lax
import numpy as np

D_MODEL = 1024
BATCH = 1
SEQ = 256
DEPTH = 1

CHUNK = 64
CONV_DIM = D_MODEL
CONV_WIDTH = 31
GLA_HEADS = 4
GLA_DK = D_MODEL // 2
GLA_DV = D_MODEL
GLA_HK = GLA_DK // GLA_HEADS
GLA_HV = GLA_DV // GLA_HEADS
GATE_RANK = 16
GATE_TAU = 16.0
N_GROUPS = 8
EXPERTS_PER_GROUP = 8
N_EXPERTS = N_GROUPS * EXPERTS_PER_GROUP
TOP_K = 2
D_EXPERT = D_MODEL // 2
MOE_BLOCK = 128
LN_EPS = 1e-5
RMS_EPS = 1e-6
DEEPNORM_ALPHA = (2.0 * DEPTH) ** 0.25
DEEPNORM_BETA = (8.0 * DEPTH) ** -0.25
IN_SPLITS = (CONV_DIM, CONV_DIM, GLA_DK, GLA_DK, GLA_DV, GLA_DV, GATE_RANK, D_MODEL, D_MODEL)
D_IN_PROJ = sum(IN_SPLITS)


def layer_norm(x, g, b):
    xf = x.astype(jnp.float32)
    mu = jnp.mean(xf, axis=-1, keepdims=True)
    var = jnp.mean(jnp.square(xf - mu), axis=-1, keepdims=True)
    return ((xf - mu) * lax.rsqrt(var + LN_EPS) * g + b).astype(x.dtype)

def conv_module(a, g, conv_w, conv_b, ln_g, ln_b, w_co, b_co):
    u = a * jax.nn.sigmoid(g)
    u = lax.conv_general_dilated(
        u, conv_w[:, None, :].astype(u.dtype), window_strides=(1,),
        padding=[(CONV_WIDTH - 1, 0)],
        dimension_numbers=("NWC", "WIO", "NWC"),
        feature_group_count=CONV_DIM) + conv_b
    u = jax.nn.silu(layer_norm(u, ln_g, ln_b))
    return u @ w_co + b_co

def gla_branch(q, k, v, r, f_lr, w_gate_up, b_gate_up, norm_g, w_o):
    bsz, seq, _ = q.shape
    n_chunks = seq // CHUNK
    dt = q.dtype
    f32 = jnp.float32
    log_a = jax.nn.log_sigmoid((f_lr @ w_gate_up + b_gate_up).astype(f32)) / GATE_TAU

    def chunked(t, hd):
        return t.astype(f32).reshape(bsz, n_chunks, CHUNK, GLA_HEADS, hd)

    qc = chunked(q, GLA_HK) * (GLA_HK ** -0.5)
    kc = chunked(k, GLA_HK)
    vc = chunked(v, GLA_HV)
    cum = jnp.cumsum(chunked(log_a, GLA_HK), axis=2)
    cum_end = cum[:, :, -1:]
    k_dec = kc * jnp.exp(cum_end - cum)
    chunk_kv = jnp.einsum("bnchk,bnchv->nbhkv", k_dec, vc)
    chunk_decay = jnp.exp(cum_end[:, :, 0]).transpose(1, 0, 2, 3)

    def step(state, inp):
        dec, kv = inp
        state = dec[..., None] * state + kv
        return state, state

    s0 = jnp.zeros((bsz, GLA_HEADS, GLA_HK, GLA_HV), f32)
    _, states = lax.scan(step, s0, (chunk_decay, chunk_kv))
    o = jnp.einsum("bnchk,nbhkv->bnchv", qc, states).reshape(bsz, seq, GLA_HEADS, GLA_HV)
    o = o * lax.rsqrt(jnp.mean(jnp.square(o), axis=-1, keepdims=True) + RMS_EPS) * norm_g
    o = o * jax.nn.silu(r.astype(f32)).reshape(bsz, seq, GLA_HEADS, GLA_HV)
    return o.reshape(bsz, seq, GLA_DV).astype(dt) @ w_o

def hier_moe(x, w_rg, b_rg, w_re, b_re, w1, w3, w2):
    bsz, seq, d = x.shape
    n_tok = bsz * seq
    xt = x.reshape(n_tok, d)
    f32 = jnp.float32
    g_logits = (xt @ w_rg + b_rg).astype(f32)
    g_prob = jax.nn.softmax(g_logits, axis=-1)
    _, g_sel = lax.top_k(g_logits, 1)
    g_w = jnp.take_along_axis(g_prob, g_sel, axis=1)
    e_all = (xt @ w_re + b_re).astype(f32).reshape(n_tok, N_GROUPS, EXPERTS_PER_GROUP)
    e_logits = jnp.take_along_axis(e_all, g_sel[:, :, None], axis=1)[:, 0]
    top_v, top_i = lax.top_k(e_logits, TOP_K)
    weights = g_w * jax.nn.softmax(top_v, axis=-1)
    expert = g_sel * EXPERTS_PER_GROUP + top_i

    n_assign = n_tok * TOP_K
    flat_e = expert.reshape(-1)
    flat_tok = jnp.repeat(jnp.arange(n_tok, dtype=jnp.int32), TOP_K)
    flat_w = weights.reshape(-1)
    order = jnp.argsort(flat_e)
    se, st, sw = flat_e[order], flat_tok[order], flat_w[order]
    counts = jnp.bincount(flat_e, length=N_EXPERTS)
    starts = jnp.cumsum(counts) - counts
    pcounts = (counts + MOE_BLOCK - 1) // MOE_BLOCK * MOE_BLOCK
    pends = jnp.cumsum(pcounts)
    pstarts = pends - pcounts
    dest = pstarts[se] + (jnp.arange(n_assign) - starts[se])
    n_blocks = -(-n_assign // MOE_BLOCK) + N_EXPERTS
    n_slots = n_blocks * MOE_BLOCK
    slot_tok = jnp.zeros((n_slots,), jnp.int32).at[dest].set(st)
    slot_w = jnp.zeros((n_slots,), x.dtype).at[dest].set(sw.astype(x.dtype))
    block_e = jnp.minimum(
        jnp.searchsorted(pends, jnp.arange(n_blocks) * MOE_BLOCK, side="right"), N_EXPERTS - 1)
    xs = xt[slot_tok].reshape(n_blocks, MOE_BLOCK, d)

    def expert_block(args):
        xb, e = args
        hdn = jax.nn.silu(xb @ w1[e]) * (xb @ w3[e])
        return hdn @ w2[e]

    ys = lax.map(expert_block, (xs, block_e)).reshape(n_slots, d) * slot_w[:, None]
    out = jnp.zeros((n_tok, d), x.dtype).at[slot_tok].add(ys)
    return out.reshape(bsz, seq, d)

def first_inputs(seed: int = 0) -> dict:
    key = jax.random.key(seed)
    ks = jax.random.split(key, 26)
    L = DEPTH

    def nrm(k, shape, scale):
        return jax.random.normal(k, shape, jnp.float32) * scale

    return {
        "x": nrm(ks[0], (BATCH, SEQ, D_MODEL), 1.0),
        "w_in": nrm(ks[1], (L, D_MODEL, D_IN_PROJ), D_MODEL ** -0.5),
        "b_in": nrm(ks[2], (L, D_IN_PROJ), 0.02),
        "conv_w": nrm(ks[3], (L, CONV_WIDTH, CONV_DIM), CONV_WIDTH ** -0.5),
        "conv_b": nrm(ks[4], (L, CONV_DIM), 0.02),
        "conv_ln_g": 1.0 + nrm(ks[5], (L, CONV_DIM), 0.05),
        "conv_ln_b": nrm(ks[6], (L, CONV_DIM), 0.02),
        "w_conv_out": nrm(ks[7], (L, CONV_DIM, D_MODEL), CONV_DIM ** -0.5),
        "b_conv_out": nrm(ks[8], (L, D_MODEL), 0.02),
        "w_gate_up": nrm(ks[9], (L, GATE_RANK, GLA_DK), GATE_RANK ** -0.5),
        "b_gate_up": nrm(ks[10], (L, GLA_DK), 0.1),
        "gla_norm_g": 1.0 + nrm(ks[11], (L, GLA_HEADS, GLA_HV), 0.05),
        "w_gla_out": nrm(ks[12], (L, GLA_DV, D_MODEL), GLA_DV ** -0.5),
        "w_out": nrm(ks[13], (L, D_MODEL, D_MODEL), D_MODEL ** -0.5 * DEEPNORM_BETA),
        "b_out": nrm(ks[14], (L, D_MODEL), 0.02),
        "ln1_g": 1.0 + nrm(ks[15], (L, D_MODEL), 0.05),
        "ln1_b": nrm(ks[16], (L, D_MODEL), 0.02),
        "w_router_group": nrm(ks[17], (L, D_MODEL, N_GROUPS), D_MODEL ** -0.5),
        "b_router_group": nrm(ks[18], (L, N_GROUPS), 0.01),
        "w_router_expert": nrm(ks[19], (L, D_MODEL, N_EXPERTS), D_MODEL ** -0.5),
        "b_router_expert": nrm(ks[20], (L, N_EXPERTS), 0.01),
        "w1": nrm(ks[21], (L, N_EXPERTS, D_MODEL, D_EXPERT), D_MODEL ** -0.5),
        "w3": nrm(ks[22], (L, N_EXPERTS, D_MODEL, D_EXPERT), D_MODEL ** -0.5),
        "w2": nrm(ks[23], (L, N_EXPERTS, D_EXPERT, D_MODEL), D_EXPERT ** -0.5 * DEEPNORM_BETA),
        "ln2_g": 1.0 + nrm(ks[24], (L, D_MODEL), 0.05),
        "ln2_b": nrm(ks[25], (L, D_MODEL), 0.02),
    }

def first_block(x, w_in, b_in, conv_w, conv_b, conv_ln_g, conv_ln_b, w_conv_out, b_conv_out,
              w_gate_up, b_gate_up, gla_norm_g, w_gla_out, w_out, b_out, ln1_g, ln1_b,
              w_router_group, b_router_group, w_router_expert, b_router_expert,
              w1, w3, w2, ln2_g, ln2_b):
    split_points = np.cumsum(IN_SPLITS)[:-1].tolist()
    for l in range(DEPTH):
        h = x @ w_in[l] + b_in[l]
        conv_a, conv_g, q, k, v, r, f_lr, gate_a, gate_b = jnp.split(h, split_points, axis=-1)
        y_conv = conv_module(conv_a, conv_g, conv_w[l], conv_b[l], conv_ln_g[l], conv_ln_b[l],
                             w_conv_out[l], b_conv_out[l])
        y_gla = gla_branch(q, k, v, r, f_lr, w_gate_up[l], b_gate_up[l], gla_norm_g[l], w_gla_out[l])
        merged = jax.nn.sigmoid(gate_a) * y_conv + jax.nn.sigmoid(gate_b) * y_gla
        mix = merged @ w_out[l] + b_out[l]
        x = layer_norm(DEEPNORM_ALPHA * x + mix, ln1_g[l], ln1_b[l])
        ffn = hier_moe(x, w_router_group[l], b_router_group[l], w_router_expert[l],
                       b_router_expert[l], w1[l], w3[l], w2[l])
        x = layer_norm(DEEPNORM_ALPHA * x + ffn, ln2_g[l], ln2_b[l])
    return x


N_BRANCH = 4
BRANCH_W = D_MODEL // N_BRANCH
NEG_BIG = -1e30
LOG_FLOOR = 1e-30
HG_HEADS = 4
HG_DK = 128
HG_DV = BRANCH_W // HG_HEADS
POOL_WINDOWS = (2, 4, 8, 16)
POOL_GROUP = BRANCH_W // len(POOL_WINDOWS)
SA_HEADS = 4
SA_DH = BRANCH_W // SA_HEADS
IDX_HEADS = 8
IDX_DH = 64
TOPK_MAX = 256
Q_BLOCK = 128
N_MEM = 256
MEM_HEADS = 4
MEM_DH = BRANCH_W // MEM_HEADS
D_FF = -(-8 * D_MODEL // (3 * 256)) * 256
SPLIT_SIZES = (HG_HEADS * HG_DK, HG_HEADS * HG_DK, BRANCH_W, BRANCH_W,
               BRANCH_W,
               SA_HEADS * SA_DH, SA_DH, SA_DH,
               IDX_HEADS * IDX_DH, IDX_DH, IDX_HEADS,
               MEM_HEADS * MEM_DH)
N_IN = sum(SPLIT_SIZES)


F32 = jnp.float32

def rms_norm(x, gain, eps=RMS_EPS):
    xf = x.astype(F32)
    y = xf * lax.rsqrt(jnp.mean(xf * xf, axis=-1, keepdims=True) + eps)
    return (y * gain.astype(F32)).astype(x.dtype)

def hgrn2_mixer(q, f_logit, i, g, lb, o_gain):
    B, T, _ = q.shape
    n = T // CHUNK
    lbf = lb.astype(F32)
    sg = jax.nn.sigmoid(f_logit.astype(F32))
    f = lbf + (1.0 - lbf) * sg
    log_f = jnp.log(jnp.maximum(f, LOG_FLOOR))
    k = (1.0 - lbf) * (1.0 - sg)
    qf = jax.nn.silu(q.astype(F32))

    def to_chunks(a, d):
        return a.reshape(B, n, CHUNK, HG_HEADS, d).transpose(1, 0, 2, 3, 4)

    xs = (to_chunks(qf, HG_DK), to_chunks(k, HG_DK), to_chunks(log_f, HG_DK),
          to_chunks(i.astype(F32), HG_DV))
    causal = jnp.tril(jnp.ones((CHUNK, CHUNK), dtype=bool))[None, :, :, None, None]

    def step(S, inp):
        qc, kc, lfc, vc = inp
        b = jnp.cumsum(lfc, axis=1)
        o_inter = jnp.einsum('bthk,bhkv->bthv', qc * jnp.exp(b), S)
        diff = jnp.where(causal, b[:, :, None] - b[:, None, :], 0.0)
        decay = jnp.where(causal, jnp.exp(diff), 0.0)
        att = jnp.einsum('bthk,bshk,btshk->bhts', qc, kc, decay)
        o_intra = jnp.einsum('bhts,bshv->bthv', att, vc)
        b_last = b[:, -1]
        S = jnp.exp(b_last)[..., None] * S + jnp.einsum(
            'bshk,bshv->bhkv', kc * jnp.exp(b_last[:, None] - b), vc)
        return S, o_inter + o_intra

    S0 = jnp.zeros((B, HG_HEADS, HG_DK, HG_DV), F32)
    _, o = lax.scan(step, S0, xs)
    o = o.transpose(1, 0, 2, 3, 4).reshape(B, T, HG_HEADS, HG_DV)
    o = o * lax.rsqrt(jnp.mean(o * o, axis=-1, keepdims=True) + RMS_EPS)
    o = o.reshape(B, T, BRANCH_W) * o_gain.astype(F32) * jax.nn.silu(g.astype(F32))
    return o.astype(q.dtype)

def pool_mixer(z, pool_w, pool_scale):
    B, T, _ = z.shape
    zf = z.astype(F32).reshape(B, T, len(POOL_WINDOWS), POOL_GROUP)
    csum = jnp.cumsum(zf, axis=1)
    pos = jnp.arange(T)
    means = []
    for gi, w in enumerate(POOL_WINDOWS):
        c = csum[:, :, gi]
        lagged = jnp.pad(c, ((0, 0), (w, 0), (0, 0)))[:, :T]
        cnt = jnp.minimum(pos + 1, w).astype(F32)
        means.append((c - lagged) / cnt[None, :, None])
    pooled = jnp.stack(means, axis=2) - zf
    y = jnp.einsum('btgc,gcd->btgd', pooled, pool_w.astype(F32)).reshape(B, T, BRANCH_W)
    return (y * pool_scale.astype(F32)).astype(z.dtype)

def dsa_mixer(q, k, v, iq, ik, iw):
    B, T, _ = q.shape
    n_sel = min(TOPK_MAX, T // 4)
    nb = T // Q_BLOCK

    def blocks(a, tail):
        return jnp.moveaxis(a.reshape((B, nb, Q_BLOCK) + tail), 1, 0)

    qb_all = blocks(q, (SA_HEADS, SA_DH))
    iqb_all = blocks(iq, (IDX_HEADS, IDX_DH))
    iwb_all = blocks(iw, (IDX_HEADS,))
    key_pos = jnp.arange(T)
    gather = jax.vmap(lambda arr, idx: arr[idx])

    def block(args):
        bi, qb, iqb, iwb = args
        qpos = bi * Q_BLOCK + jnp.arange(Q_BLOCK)
        limit = (qpos // CHUNK + 1) * CHUNK
        admissible = key_pos[None, :] < limit[:, None]
        logits = jnp.einsum('bqhd,bsd->bqsh', iqb, ik).astype(F32) * (IDX_DH ** -0.5)
        score = jnp.einsum('bqsh,bqh->bqs', jax.nn.relu(logits),
                           iwb.astype(F32) * (IDX_HEADS ** -0.5))
        score = jnp.where(admissible[None], score, NEG_BIG)
        top_val, top_idx = lax.top_k(score, n_sel)
        valid = top_val > 0.5 * NEG_BIG
        k_sel = gather(k, top_idx)
        v_sel = gather(v, top_idx)
        s = jnp.einsum('bqhd,bqkd->bhqk', qb, k_sel).astype(F32) * (SA_DH ** -0.5)
        s = jnp.where(valid[:, None], s, NEG_BIG)
        p = jax.nn.softmax(s, axis=-1)
        o = jnp.einsum('bhqk,bqkd->bqhd', p.astype(v.dtype), v_sel)
        return o.reshape(B, Q_BLOCK, SA_HEADS * SA_DH)

    out = lax.map(block, (jnp.arange(nb), qb_all, iqb_all, iwb_all))
    return jnp.moveaxis(out, 0, 1).reshape(B, T, SA_HEADS * SA_DH)

def mem_attention(qm, mk, mv):
    B, T, _ = qm.shape
    qh = qm.reshape(B, T, MEM_HEADS, MEM_DH)
    kh = mk.reshape(B, N_MEM, MEM_HEADS, MEM_DH)
    vh = mv.reshape(B, N_MEM, MEM_HEADS, MEM_DH)
    s = jnp.einsum('bthd,bnhd->bhtn', qh, kh).astype(F32) * (MEM_DH ** -0.5)
    p = jax.nn.softmax(s, axis=-1)
    o = jnp.einsum('bhtn,bnhd->bthd', p.astype(vh.dtype), vh)
    return o.reshape(B, T, MEM_HEADS * MEM_DH)

def second_inputs(seed: int = 0) -> dict:
    key = jax.random.key(seed)
    ks = jax.random.split(key, 18)
    L, D = DEPTH, D_MODEL
    nrm = lambda k, shape, fan: jax.random.normal(k, shape, F32) * (fan ** -0.5)
    gain = lambda k, shape: 1.0 + 0.1 * jax.random.normal(k, shape, F32)
    return {
        "x": jax.random.normal(ks[0], (BATCH, SEQ, D), F32),
        "mem": jax.random.normal(ks[1], (BATCH, N_MEM, D), F32),
        "lb_logits": jax.random.normal(ks[2], (L, HG_HEADS * HG_DK), F32),
        "w_in": nrm(ks[3], (L, D, N_IN), D),
        "w_gate": nrm(ks[4], (L, N_BRANCH, D, D), D),
        "w_branch": nrm(ks[5], (L, N_BRANCH, BRANCH_W, D), BRANCH_W),
        "w_out": nrm(ks[6], (L, D, D), D),
        "hgrn_norm": gain(ks[7], (L, BRANCH_W)),
        "pool_w": nrm(ks[8], (L, len(POOL_WINDOWS), POOL_GROUP, POOL_GROUP), POOL_GROUP),
        "pool_scale": gain(ks[9], (L, BRANCH_W)),
        "w_mem_kv": nrm(ks[10], (L, D, 2 * MEM_HEADS * MEM_DH), D),
        "norm_mem": gain(ks[11], (L, D)),
        "norm_mix_pre": gain(ks[12], (L, D)),
        "norm_mix_post": gain(ks[13], (L, D)),
        "norm_ffn_pre": gain(ks[14], (L, D)),
        "norm_ffn_post": gain(ks[15], (L, D)),
        "w_ffn_gate_up": nrm(ks[16], (L, D, 2 * D_FF), D),
        "w_ffn_down": nrm(ks[17], (L, D_FF, D), D_FF),
    }

def second_block(x, mem, lb_logits, w_in, w_gate, w_branch, w_out, hgrn_norm, pool_w,
              pool_scale, w_mem_kv, norm_mem, norm_mix_pre, norm_mix_post,
              norm_ffn_pre, norm_ffn_post, w_ffn_gate_up, w_ffn_down):
    split_pts = [int(p) for p in np.cumsum(SPLIT_SIZES)[:-1]]
    lb_soft = jax.nn.softmax(lb_logits.astype(F32), axis=0)
    lb_all = jnp.cumsum(lb_soft, axis=0) - lb_soft[0:1]
    h = x
    for l in range(DEPTH):
        u = rms_norm(h, norm_mix_pre[l])
        z = u @ w_in[l]
        (hq, hf, hi, hg, pz, sq, sk, sv, iq, ik, iw, mq) = jnp.split(z, split_pts, axis=-1)
        y_a = hgrn2_mixer(hq, hf, hi, hg, lb_all[l], hgrn_norm[l])
        y_b = pool_mixer(pz, pool_w[l], pool_scale[l])
        y_c = dsa_mixer(sq, sk, sv, iq, ik, iw)
        mkv = rms_norm(mem, norm_mem[l]) @ w_mem_kv[l]
        mk, mv = jnp.split(mkv, 2, axis=-1)
        y_m = mem_attention(mq, mk, mv)
        merged = None
        for bi, y in enumerate((y_a, y_b, y_c, y_m)):
            term = jax.nn.sigmoid(u @ w_gate[l, bi]) * (y @ w_branch[l, bi])
            merged = term if merged is None else merged + term
        h = h + rms_norm(merged @ w_out[l], norm_mix_post[l])
        u = rms_norm(h, norm_ffn_pre[l])
        gt, up = jnp.split(u @ w_ffn_gate_up[l], 2, axis=-1)
        h = h + rms_norm((jax.nn.silu(gt) * up) @ w_ffn_down[l], norm_ffn_post[l])
    return h


def setup_inputs(seed=0):
    out = dict(first_inputs(seed))
    for name, value in second_inputs(seed + 1).items():
        if name != "x":
            out[name + "_2"] = value
    return out


def reference(
    x, w_in, b_in, conv_w, conv_b, conv_ln_g, conv_ln_b, w_conv_out, b_conv_out, w_gate_up,
    b_gate_up, gla_norm_g, w_gla_out, w_out, b_out, ln1_g, ln1_b, w_router_group,
    b_router_group, w_router_expert, b_router_expert, w1, w3, w2, ln2_g, ln2_b, mem_2,
    lb_logits_2, w_in_2, w_gate_2, w_branch_2, w_out_2, hgrn_norm_2, pool_w_2, pool_scale_2,
    w_mem_kv_2, norm_mem_2, norm_mix_pre_2, norm_mix_post_2, norm_ffn_pre_2, norm_ffn_post_2,
    w_ffn_gate_up_2, w_ffn_down_2,
):
    x = first_block(
        x, w_in, b_in, conv_w, conv_b, conv_ln_g, conv_ln_b, w_conv_out, b_conv_out, w_gate_up,
        b_gate_up, gla_norm_g, w_gla_out, w_out, b_out, ln1_g, ln1_b, w_router_group,
        b_router_group, w_router_expert, b_router_expert, w1, w3, w2, ln2_g, ln2_b,
    )
    return second_block(
        x, mem_2, lb_logits_2, w_in_2, w_gate_2, w_branch_2, w_out_2, hgrn_norm_2, pool_w_2,
        pool_scale_2, w_mem_kv_2, norm_mem_2, norm_mix_pre_2, norm_mix_post_2, norm_ffn_pre_2,
        norm_ffn_post_2, w_ffn_gate_up_2, w_ffn_down_2,
    )


_drawn_inputs = setup_inputs


def setup_inputs(seed=0):
    import zlib

    import numpy as np

    out = dict(_drawn_inputs(seed))
    spreads = {}
    factors = {'b_in': 2.784,
     'conv_b': 3.034,
     'conv_ln_b': 4.501,
     'b_conv_out': 3.788,
     'b_gate_up': 2.757,
     'gla_norm_g': 2.8,
     'b_router_group': 5.668,
     'b_router_expert': 5.751,
     'norm_mem_2': 4.41}
    for name, (base, spread) in spreads.items():
        noise = np.random.default_rng([zlib.crc32(name.encode()), seed]).standard_normal(out[name].shape)
        drawn = base * np.exp(spread * noise) if base else spread * noise
        out[name] = __import__('jax').numpy.asarray(drawn.astype(out[name].dtype))
    for name, factor in factors.items():
        out[name] = (out[name] * factor).astype(out[name].dtype)
    return out
```

```python
from contextlib import ExitStack

import numpy as np

import concourse.bass as bass
from concourse import mybir

F32 = mybir.dt.float32
I32 = mybir.dt.int32
ALU = mybir.AluOpType
ACT = mybir.ActivationFunctionType
AX = mybir.AxisListType.X

P = 128
T = 256
TT = T // P
D = 1024
DT = D // P
CHUNK = 64
NC = T // CHUNK
CW = 31
PAD = CW - 1
GH = 4
GDK, GDV, RANK = 512, 1024, 16
NG, EPG, NE = 8, 8, 64
DE = 512
ET = DE // P
SLOTS = 32
QUAD = 4
NQ = NE // QUAD
ROUNDS = T // SLOTS
HH, HDV = 4, 64
AH, ADH = 4, 64
IH = 8
FF = 2816
FT = FF // P
NSEL = 64
SLOT_COLS = 4096
RING = 6
RING2 = 4
LN_EPS, RMS_EPS = 1e-5, 1e-6
ALPHA1 = 2.0 ** 0.25
BIG = 1e30

O_A, O_G, O_Q, O_K, O_V, O_R, O_F = 0, 1024, 2048, 2560, 3072, 4096, 5120
O_GA, O_GB = 5136, 6160
Z_HQ, Z_HF, Z_HI, Z_PZ, Z_SK, Z_IQ3 = 0, 512, 1024, 1536, 2048, 2560
N_IN2 = 3016

VEC_SIZES = dict(b_a=8, b_g=8, b_q=4, b_r=8, b_f=1, b_ga=8, b_gb=8, conv_w=8 * CW, conv_b=8, cln_g=8,
                 cln_b=8, b_co=8, gla_g=8, b_out=8, ln1_g=8, ln1_b=8, ln2_g=8, ln2_b=8, lb=4,
                 hg_g=2, pool_s=2, n_mem=8, n_mix_pre=8, n_mix_post=8, n_ffn_pre=8, n_ffn_post=8)
ROW_SIZES = dict(b_k=512, b_v=1024, b_rt=NG + NE)
CONST_SIZES = dict(ident=P, after=P, before=P, ones=P, j1024=P, j256=P, j64=P, chunk_of=2,
                   slot_iota=SLOTS, ln_eps=1, rms_eps=1, rounds=ROUNDS, rank8=NG, rank64=NE)
CONST2_SIZES = dict(level=7 * P, inv_count=2 * T, not_adm=TT * T)
LEVELS = 7


def columns(sizes):
    at, out = 0, {}
    for name, n in sizes.items():
        out[name] = (at, n)
        at += n
    return out, at


VEC, NVEC = columns(VEC_SIZES)
ROW, NROW = columns(ROW_SIZES)
CON, NCON = columns(CONST_SIZES)
CON2, NCON2 = columns(CONST2_SIZES)


def constants():
    i = np.arange(P)
    s, t = i[:, None], i[None, :]
    c = np.zeros((P, NCON), np.float32)
    put = lambda n, v: c.__setitem__((slice(None), slice(CON[n][0], sum(CON[n]))), v)
    put("ident", s == t)
    put("after", (s > t) & (s // CHUNK == t // CHUNK))
    put("before", s < t)
    put("ones", 1.0)
    put("j1024", 1.0 / D)
    put("j256", 1.0 / T)
    put("j64", (s // HDV == t // HDV) / HDV)
    put("chunk_of", s // CHUNK == np.arange(2)[None, :])
    put("slot_iota", np.arange(SLOTS)[None, :])
    put("rounds", SLOTS * np.arange(ROUNDS)[None, :])
    put("ln_eps", LN_EPS)
    put("rms_eps", RMS_EPS)
    put("rank8", NG - np.arange(NG)[None, :])
    put("rank64", NE - np.arange(NE)[None, :])
    d = np.zeros((P, NCON2), np.float32)
    for n in range(LEVELS - 1):
        h = 32 >> n
        m = (s // (2 * h) == t // (2 * h)) & (s % (2 * h) < h) & (t % (2 * h) >= h)
        d[:, n * P:(n + 1) * P] = m
    d[:, 6 * P:7 * P] = s == t
    for g, w in enumerate((2, 4, 8, 16)):
        a = CON2["inv_count"][0] + T * (g // 2)
        d[64 * (g % 2):64 * (g % 2) + 64, a:a + T] = 1.0 / np.minimum(np.arange(T) + 1, w)
    for tile in range(TT):
        q = tile * P + i
        a = CON2["not_adm"][0] + T * tile
        d[:, a:a + T] = np.where(np.arange(T)[None, :] < ((q // CHUNK + 1) * CHUNK)[:, None], 0.0, -BIG)
    return c, d


class Banks:

    def __init__(self, sem, name):
        self.full = [sem(f"{name}_full{b}") for b in range(8)]
        self.free = [sem(f"{name}_free{b}") for b in range(8)]
        self.uses, self.place, self.turn = [0] * 8, {}, 0

    def take(self, pe, group):
        b = self.turn % 8
        self.turn += 1
        if self.uses[b]:
            pe.wait_ge(self.free[b], self.uses[b])
        self.uses[b] += 1
        self.place[group] = (b, self.uses[b])
        return b

    def wait_full(self, eng, group):
        b, n = self.place[group]
        eng.wait_ge(self.full[b], n)
        return b

    def wait_read(self, eng, group):
        b, n = self.place[group]
        eng.wait_ge(self.free[b], n)

    def free_of(self, group):
        return self.free[self.place[group][0]]


class Ring:

    def __init__(self, sem, name, slabs, slots):
        self.slots = slots
        self.landed = [sem(f"{name}_landed{s}") for s in range(slots)]
        self.slabs, self.last_group = slabs, {}
        self.index = {s: i for i, s in enumerate(slabs)}
        self.count = {}
        for i, s in enumerate(slabs):
            before = self.count[slabs[i - slots]] if i >= slots else 0
            self.count[s] = before + 16 * (2 if s.startswith("br") else 1)

    def wait_landed(self, pe, slab):
        pe.wait_ge(self.landed[self.slot(slab)], self.count[slab])
        return self.slot(slab)

    def slot(self, slab):
        return self.index[slab] % self.slots

    def load(self, sp, banks, slab, dst, src):
        self.wait_free(sp, banks, slab)
        sp.dma_start(dst, src).then_inc(self.landed[self.slot(slab)], 16)

    def wait_free(self, sp, banks, slab):
        i = self.index[slab]
        if i >= self.slots:
            banks.wait_full(sp, self.last_group[self.slabs[i - self.slots]])


class Line:

    def __init__(self, eng):
        self.eng, self.count = eng, {}

    def done(self, ins, sem):
        ins.then_inc(sem, 1)
        self.count[sem.name] = self.count.get(sem.name, 0) + 1
        self.eng.wait_ge(sem, self.count[sem.name])

    def read(self, ins, banks, group):
        ins.then_inc(banks.free_of(group), 1)
        banks.wait_read(self.eng, group)


SLABS1 = ["a0", "g0", "a1", "g1", "k", "q", "v0", "v1", "r0", "r1", "ga0", "ga1", "gb0", "gb1",
          "co0", "co1", "go0", "go1", "wo0", "wo1"]
SLABS2 = (["mem", "z0", "z1", "z2", "z3", "z4", "z5", "gate1_0", "gate1_1", "gate3_0", "gate3_1", "br13",
           "gate0_0", "gate0_1", "br02", "gate2_0", "gate2_1", "o0", "o1"]
          + [f"ff{i}" for i in range(11)] + [f"dn{i}" for i in range(6)])
IN_COLS = dict(a0=O_A, a1=O_A + 512, g0=O_G, g1=O_G + 512, k=O_K, q=O_Q, v0=O_V, v1=O_V + 512,
               r0=O_R, r1=O_R + 512, ga0=O_GA, ga1=O_GA + 512, gb0=O_GB, gb1=O_GB + 512)


class Chip:

    def __init__(self, nc, ctx, d):
        self.nc, self.ctx, self.d = nc, ctx, d
        self.names, self.lines = {}, {}
        sb = lambda name, cols, dt=F32: ctx.enter_context(nc.sbuf_tensor(name, [P, cols], dt))
        self.ring = sb("ring", RING * SLOT_COLS)
        self.arena = sb("arena", 12 * 2048)
        self.con = sb("con", NCON)
        self.vec = sb("vec", NVEC)
        self.wf = sb("wf", DT * RANK)
        self.small = sb("small", GH * NC)
        self.rowbuf = sb("rowbuf", DT * T)
        self.rounds_int = sb("rounds_int", 1, I32)
        self.psum = ctx.enter_context(nc.psum_tensor("psum", [P, 8, 512], F32))
        self.banks1 = Banks(self.sem, "bank1")
        self.banks2 = Banks(self.sem, "bank2")
        self.ring1 = Ring(self.sem, "ring1", SLABS1, RING)
        self.ring2 = Ring(self.sem, "ring2", SLABS2, RING2)

    def sem(self, name):
        if name not in self.names:
            self.names[name] = self.ctx.enter_context(self.nc.semaphore(name))
        return self.names[name]

    def line(self, name, eng):
        return self.lines.setdefault(name, Line(eng))

    def A(self, slot, cols=2048, at=0):
        if slot >= 12:
            a = RING2 * SLOT_COLS + (slot - 12) * 2048 + at
            return self.ring[:, a:a + cols]
        return self.arena[:, slot * 2048 + at:slot * 2048 + at + cols]

    def tiles(self, slot, n, w=T, at=0):
        return self.A(slot, n * w, at).rearrange("p (k t) -> p k t", k=n)

    def c(self, name):
        a, n = CON[name]
        return self.con[:, a:a + n]

    def c2(self, name):
        a, n = CON2[name]
        return self.A(11, n, a)

    def v(self, name, i=0, n=1):
        a = VEC[name][0] + i
        return self.vec[:, a:a + n]

    def row(self, name, at=0, n=None):
        a, m = ROW[name]
        return self.rowbuf[32:33, a + at:a + at + (m if n is None else n)]

    def w_gate_up(self):
        return self.rowbuf[0:RANK + 1, 0:GDK]

    def f_low(self, rows=RANK):
        return self.rowbuf[0:rows, GDK:GDK + T]

    def chunk_decay(self):
        return self.small[:, 0:GH * NC]

    def rstd(self, i):
        return self.A(2, T, 1024 if i == 3 else 240 + T * i)

    def slab(self, slot, k=DT):
        w = SLOT_COLS // k
        return self.ring[:, slot * SLOT_COLS:(slot + 1) * SLOT_COLS].rearrange("p (k n) -> p k n", k=k)



def pe_group(K, pe, banks, group, weights, acts, out=(slice(0, P), slice(0, T)), bias=None):
    b = banks.take(pe, group)
    o = K.psum[out[0], b, out[1]]
    n = len(weights)
    for k in range(n):
        m = pe.matmul(o, weights[k], acts[k], start=(k == 0), stop=(k == n - 1 and bias is None))
    if bias is not None:
        m = pe.matmul(o, K.con[32:33, CON["ones"][0]:CON["ones"][0] + P], bias, start=False, stop=True)
    m.then_inc(banks.full[b], 1)


def pe_slab_tiles(K, pe, banks, ring, slab, groups, acts, first=0, last=True):
    w = K.slab(ring.wait_landed(pe, slab))
    for m, group in enumerate(groups):
        c = (first + m) * P
        pe_group(K, pe, banks, group, [w[:, k, c:c + P] for k in range(DT)], [acts[:, k, :] for k in range(DT)])
    if last:
        ring.last_group[slab] = groups[-1]


def act_std(K, line, banks, group, out, eps):
    b = banks.wait_full(line.eng, group)
    line.read(line.eng.activation(out, K.psum[:, b, 0:T], ACT.Sqrt, bias=K.c(eps)), banks, group)


def dve_rstd(K, line, banks, group, out):
    banks.wait_read(line.eng, group)
    line.done(line.eng.reciprocal(out, out), K.sem("reciprocals"))


def wide(ap, n):
    p, w = ap.shape
    return ap.unsqueeze(1).to_broadcast([p, n, w])



def upad(K):
    return K.arena[:, 2048:2048 + DT * (T + PAD)].rearrange("p (k t) -> p k t", k=DT)


def block1_pe(K, pe):
    B, R, S = K.banks1, K.ring1, K.sem
    x = K.tiles(0, DT)
    tiles = lambda name, a, n: [f"{name}{m}" for m in range(a, a + n)]
    q = K.tiles(5, GH)
    k = K.tiles(5, TT, GDK, GH * T)
    v = K.tiles(6, TT, GDV)
    la = K.tiles(10, TT, GDK)
    kdec = K.tiles(10, TT, GDK, TT * GDK)
    state = K.tiles(2, GH, 256, 1024)

    pe.wait_ge(S("x_in"), 16)
    for slab, name, a in (("a0", "a", 0), ("g0", "g", 0), ("a1", "a", 4), ("g1", "g", 4)):
        pe_slab_tiles(K, pe, B, R, slab, tiles(name, a, 4), x)
    pe.wait_ge(S("params_in"), 80)
    wf = K.wf[:, :].rearrange("p (k r) -> p k r", k=DT)
    pe_group(K, pe, B, "f", [wf[:, j, :] for j in range(DT)], [x[:, j, :] for j in range(DT)],
             out=(slice(0, RANK), slice(0, T)))

    def rows(slab, name, bias):
        w = K.slab(R.wait_landed(pe, slab))
        for t in range(TT):
            pe_group(K, pe, B, f"{name}_{t}", [x[:, j, t * P:(t + 1) * P] for j in range(DT)],
                     [w[:, j, :] for j in range(DT)], out=(slice(0, P), slice(0, 512)), bias=bias)
        R.last_group[slab] = f"{name}_{TT - 1}"

    row = K.row
    rows("k", "k", row("b_k"))
    pe_slab_tiles(K, pe, B, R, "q", tiles("q", 0, 4), x)
    B.wait_read(pe, "f")
    for t in range(TT):
        pe_group(K, pe, B, f"z_{t}", [K.f_low(RANK + 1)[:, t * P:(t + 1) * P]], [K.w_gate_up()],
                 out=(slice(0, P), slice(0, 512)))
    rows("v0", "v0", row("b_v", 0, 512))
    rows("v1", "v1", row("b_v", 512, 512))
    for slab, name, a in (("r0", "r", 0), ("r1", "r", 4), ("ga0", "ga", 0), ("ga1", "ga", 4), ("gb0", "gb", 0)):
        pe_slab_tiles(K, pe, B, R, slab, tiles(name, a, 4), x)

    pe.wait_ge(S("log_decay"), TT)
    for t in range(TT):
        pe_group(K, pe, B, f"later_{t}", [K.c("after")], [la[:, t, :]], out=(slice(0, P), slice(0, 512)))
    b = B.take(pe, "chunk_sum")
    for h in range(GH):
        for t in range(TT):
            o = K.psum[:, b, h * NC + 2 * t:h * NC + 2 * t + 2]
            m = pe.matmul(o, la[:, t, h * P:(h + 1) * P], K.c("chunk_of"), start=True, stop=True)
    m.then_inc(B.full[b], 1)
    pe.wait_ge(S("conv_sum"), 1)
    conv, squares = K.tiles(3, DT), K.tiles(1, DT)
    pe_group(K, pe, B, "conv_mean", [K.c("j1024")] * DT, [conv[:, j, :] for j in range(DT)])
    pe_slab_tiles(K, pe, B, R, "gb1", tiles("gb", 4, 4), x)
    pe.wait_ge(S("conv_squares"), 1)
    pe_group(K, pe, B, "conv_var", [K.c("j1024")] * DT, [squares[:, j, :] for j in range(DT)])

    pe.wait_ge(S("keys_decayed"), 1)
    for c in range(NC):
        t, r = c // 2, slice(CHUNK * (c % 2), CHUNK * (c % 2) + CHUNK)
        for pair in range(2):
            b = B.take(pe, f"kv{c}_{pair}")
            for h in (2 * pair, 2 * pair + 1):
                m = pe.matmul(K.psum[:, b, 256 * (h % 2):256 * (h % 2) + 256], kdec[r, t, h * P:(h + 1) * P],
                              v[r, t, 256 * h:256 * h + 256], start=True, stop=True)
            m.then_inc(B.full[b], 1)
        pe.wait_ge(S("state"), c + 1)
        b = B.take(pe, f"o{c}")
        for h in range(GH):
            for half in range(2):
                m = pe.matmul(K.psum[:, b, (2 * h + half) * CHUNK:(2 * h + half + 1) * CHUNK],
                              state[:, h, half * P:(half + 1) * P], q[:, h, c * CHUNK:(c + 1) * CHUNK],
                              start=True, stop=True)
        m.then_inc(B.full[b], 1)

    pe.wait_ge(S("conv_act"), DT)
    cu = K.tiles(4, DT)
    for s in range(2):
        pe_slab_tiles(K, pe, B, R, f"co{s}", tiles("co", 4 * s, 4), cu)
    pe.drain().then_inc(S("moe_read0"), 1)
    pe.wait_ge(S("o_squares"), 1)
    sq = K.tiles(10, DT)
    for h in range(GH):
        pe_group(K, pe, B, f"o_ms{h}", [K.c("j256")] * 2, [sq[:, 2 * h, :], sq[:, 2 * h + 1, :]])
    pe.wait_ge(S("gla_in"), 1)
    y = K.tiles(7, DT)
    for s in range(2):
        pe_slab_tiles(K, pe, B, R, f"go{s}", tiles("go", 4 * s, 4), y)
    pe.drain().then_inc(S("moe_read1"), 1)
    pe.wait_ge(S("merged1"), 1)
    m8 = K.tiles(8, DT)
    for s in range(2):
        pe_slab_tiles(K, pe, B, R, f"wo{s}", tiles("wo", 4 * s, 4), m8)
    pe.drain().then_inc(S("moe_read2"), 1)
    pe.wait_ge(S("pre_ln1"), 1)
    h1, sq3 = K.tiles(1, DT), K.tiles(3, DT)
    pe_group(K, pe, B, "ln1_mean", [K.c("j1024")] * DT, [h1[:, j, :] for j in range(DT)])
    pe.wait_ge(S("ln1_squares"), 1)
    pe_group(K, pe, B, "ln1_var", [K.c("j1024")] * DT, [sq3[:, j, :] for j in range(DT)])


def block1_act(K, act):
    B, S, L = K.banks1, K.sem, K.line("act", act)
    ps = K.psum
    act.wait_ge(S("params_in"), 80)
    sg = K.tiles(4, DT)

    def evac(group, out, func, bias=0.0, scale=1.0, rows=slice(0, P), cols=slice(0, T)):
        b = B.wait_full(act, group)
        L.read(act.activation(out, ps[rows, b, cols], func, bias=bias, scale=scale), B, group)

    for s in range(2):
        for m in range(4 * s, 4 * s + 4):
            evac(f"g{m}", sg[:, m, :], ACT.Sigmoid, bias=K.v("b_g", m))
    act.wait_ge(S("ones_row"), 1)
    evac("f", K.f_low(), ACT.Identity, bias=K.vec[0:RANK, VEC["b_f"][0]:VEC["b_f"][0] + 1], rows=slice(0, RANK))
    k = K.tiles(5, TT, GDK, GH * T)
    v = K.tiles(6, TT, GDV)
    for t in range(TT):
        evac(f"k_{t}", k[:, t, :], ACT.Copy, cols=slice(0, 512))
    q = K.tiles(5, GH)
    for h in range(GH):
        evac(f"q{h}", q[:, h, :], ACT.Identity, bias=K.v("b_q", h))
    soft = K.tiles(10, TT, GDK)
    logit = K.tiles(10, TT, GDK, TT * GDK)
    for t in range(TT):
        evac(f"z_{t}", logit[:, t, :], ACT.Copy, cols=slice(0, 512))
        L.done(act.activation(soft[:, t, :], logit[:, t, :], ACT.Abs), S("soft_steps"))
        L.done(act.activation(soft[:, t, :], soft[:, t, :], ACT.Exp, scale=-1.0), S("soft_steps"))
        L.done(act.activation(soft[:, t, :], soft[:, t, :], ACT.Ln, bias=1.0), S("soft"))
    for n in range(2):
        for t in range(TT):
            evac(f"v{n}_{t}", v[:, t, 512 * n:512 * n + 512], ACT.Copy, cols=slice(0, 512))
    for m in range(DT):
        evac(f"r{m}", K.tiles(7, DT)[:, m, :], ACT.Silu, bias=K.v("b_r", m))
    for m in range(DT):
        evac(f"ga{m}", K.tiles(8, DT)[:, m, :], ACT.Sigmoid, bias=K.v("b_ga", m))
    for m in range(4):
        evac(f"gb{m}", K.tiles(9, DT)[:, m, :], ACT.Sigmoid, bias=K.v("b_gb", m))
    kdec = K.tiles(10, TT, GDK, TT * GDK)
    for t in range(TT):
        evac(f"later_{t}", kdec[:, t, :], ACT.Exp, scale=1.0 / 16.0, cols=slice(0, 512))
    evac("chunk_sum", K.chunk_decay(), ACT.Exp, scale=1.0 / 16.0, cols=slice(0, GH * NC))
    act.wait_ge(S("conv_centred"), 1)
    L.done(act.activation(K.A(1), K.A(3), ACT.Square), S("conv_squares"))
    for m in range(4, DT):
        evac(f"gb{m}", K.tiles(9, DT)[:, m, :], ACT.Sigmoid, bias=K.v("b_gb", m))
    o = K.tiles(11, DT)

    def out_chunk(c):
        evac(f"o{c}", o[:, :, c * CHUNK:(c + 1) * CHUNK], ACT.Copy, cols=slice(0, 512))

    act_std(K, L, B, "conv_var", K.rstd(0), "ln_eps")
    for c in range(NC):
        out_chunk(c)
    L.done(act.activation(K.A(10), K.A(11), ACT.Square), S("o_squares"))
    act.wait_ge(S("conv_normed"), 1)
    for m in range(DT):
        L.done(act.activation(K.tiles(4, DT)[:, m, :], K.tiles(3, DT)[:, m, :], ACT.Silu,
                              bias=K.v("cln_b", m), scale=K.v("cln_g", m)), S("conv_act"))
    for h in range(GH):
        act_std(K, L, B, f"o_ms{h}", K.rstd(h), "rms_eps")
    for m in range(DT):
        evac(f"wo{m}", K.tiles(1, DT)[:, m, :], ACT.Identity, bias=K.v("b_out", m))
    act.wait_ge(S("ln1_centred"), 1)
    L.done(act.activation(K.A(3), K.A(1), ACT.Square), S("ln1_squares"))
    act_std(K, L, B, "ln1_var", K.rstd(0), "ln_eps")


def block1_dve(K, dve):
    B, S, L = K.banks1, K.sem, K.line("dve", dve)
    ps = K.psum
    u = upad(K)
    L.done(dve.memset(K.f_low(RANK + 1), 1.0), S("ones_row"))
    L.done(dve.memset(u[:, :, 0:PAD], 0.0), S("pad"))
    dve.wait_ge(S("params_in"), 80)
    sg = K.tiles(4, DT)
    for m in range(DT):
        b = B.wait_full(dve, f"a{m}")
        B.wait_read(dve, f"g{m}")
        L.read(dve.scalar_tensor_tensor(u[:, m, PAD:PAD + T], ps[:, b, 0:T], K.v("b_a", m), sg[:, m, :],
                                        ALU.add, ALU.mult), B, f"a{m}")
    conv = K.tiles(3, DT)
    cw = K.v("conv_w", 0, DT * CW).rearrange("p (k w) -> p k w", k=DT)
    taps = S("taps")
    for m in range(DT):
        dve.tensor_scalar(conv[:, m, :], u[:, m, 0:T], cw[:, m, 0:1], K.v("conv_b", m), ALU.mult, ALU.add)\
           .then_inc(taps, 1)
    with dve.Fori(1, CW) as w:
        for m in range(DT):
            dve.wait_ge(taps, (w - 1) * DT + m + 1)
            dve.scalar_tensor_tensor(conv[:, m, :], u[:, m, bass.ds(w, T)], cw[:, m, bass.ds(w, 1)], conv[:, m, :],
                                     ALU.mult, ALU.add).then_inc(taps, 1)
    dve.wait_ge(taps, CW * DT)
    dve.sem_inc(S("conv_sum"), 1)
    soft = K.tiles(10, TT, GDK)
    logit = K.tiles(10, TT, GDK, TT * GDK)
    dve.wait_ge(S("soft"), TT)
    for t in range(TT):
        L.done(dve.scalar_tensor_tensor(soft[:, t, :], logit[:, t, :], 0.0, soft[:, t, :], ALU.min, ALU.subtract),
               S("log_decay"))

    q = K.A(5, GH * T)
    for h in range(GH):
        B.wait_read(dve, f"q{h}")
    L.done(dve.tensor_scalar(q, q, float(P) ** -0.5, None, ALU.mult), S("q_scaled"))

    def centre(x, group, sem):
        b = B.wait_full(dve, group)
        L.read(dve.tensor_tensor(x, x, wide(ps[:, b, 0:T], DT), ALU.subtract), B, group)
        dve.sem_inc(sem, 1)

    centre(conv, "conv_mean", S("conv_centred"))
    kdec, k = K.A(10, 1024, 1024), K.A(5, 1024, GH * T)
    for t in range(TT):
        B.wait_read(dve, f"later_{t}")
        B.wait_read(dve, f"k_{t}")
    L.done(dve.tensor_tensor(kdec, kdec, k, ALU.mult), S("keys_decayed"))
    state = K.tiles(2, GH, 256, 1024)
    B.wait_read(dve, "chunk_sum")
    dec = K.chunk_decay().rearrange("p (h c) -> p h c", h=GH)
    for c in range(NC):
        for h in range(GH):
            g = f"kv{c}_{h // 2}"
            b = B.wait_full(dve, g)
            kv = ps[:, b, 256 * (h % 2):256 * (h % 2) + 256]
            if c == 0:
                ins = dve.tensor_copy(state[:, h, :], kv)
            else:
                B.wait_full(dve, f"o{c - 1}")
                ins = dve.scalar_tensor_tensor(state[:, h, :], state[:, h, :], dec[:, h, c:c + 1], kv,
                                               ALU.mult, ALU.add)
            if h % 2:
                L.read(ins, B, g)
            else:
                L.done(ins, S("state_steps"))
        dve.sem_inc(S("state"), 1)
        if c == 0:
            r = K.rstd(0)
            dve_rstd(K, L, B, "conv_var", r)
            L.done(dve.tensor_tensor(conv, conv, wide(r, DT), ALU.mult), S("conv_normed"))
    ga, gb, o = K.tiles(8, DT), K.tiles(9, DT), K.tiles(11, DT)
    for m in range(DT):
        b = B.wait_full(dve, f"co{m}")
        L.read(dve.scalar_tensor_tensor(ga[:, m, :], ps[:, b, 0:T], K.v("b_co", m), ga[:, m, :], ALU.add, ALU.mult),
               B, f"co{m}")
    for h in range(GH):
        dve_rstd(K, L, B, f"o_ms{h}", K.rstd(h))
        for m in (2 * h, 2 * h + 1):
            L.done(dve.scalar_tensor_tensor(o[:, m, :], o[:, m, :], K.v("gla_g", m), K.rstd(h), ALU.mult, ALU.mult),
                   S("o_steps"))
    L.done(dve.tensor_tensor(K.A(7), K.A(7), K.A(11), ALU.mult), S("gla_in"))
    for m in range(DT):
        b = B.wait_full(dve, f"go{m}")
        L.read(dve.tensor_tensor(gb[:, m, :], ps[:, b, 0:T], gb[:, m, :], ALU.mult), B, f"go{m}")
    L.done(dve.tensor_tensor(K.A(8), K.A(8), K.A(9), ALU.add), S("merged1"))
    for m in range(DT):
        B.wait_read(dve, f"wo{m}")
    L.done(dve.scalar_tensor_tensor(K.A(1), K.A(0), ALPHA1, K.A(1), ALU.mult, ALU.add), S("pre_ln1"))
    centre(K.tiles(1, DT), "ln1_mean", S("ln1_centred"))
    dve_rstd(K, L, B, "ln1_var", K.rstd(0))
    L.done(dve.tensor_tensor(K.tiles(1, DT), K.tiles(1, DT), wide(K.rstd(0), DT), ALU.mult), S("ln1_steps"))
    for m in range(DT):
        L.done(dve.tensor_scalar(K.tiles(0, DT)[:, m, :], K.tiles(1, DT)[:, m, :], K.v("ln1_g", m), K.v("ln1_b", m),
                                 ALU.mult, ALU.add), S("x1"))


def block1_sp(K, sp):
    S, R, d = K.sem, K.ring1, K.d
    by_tile = lambda w: w.rearrange("(k p) n -> p k n", p=P)
    sp.dma_start(K.tiles(0, DT), by_tile(d["x"])).then_inc(S("x_in"), 16)
    w_in = by_tile(d["w_in"])

    def load(slab):
        if slab in IN_COLS:
            src = w_in[:, :, IN_COLS[slab]:IN_COLS[slab] + 512]
        else:
            w = dict(co="w_conv_out", go="w_gla_out", wo="w_out")[slab[:2]]
            src = by_tile(d[w])[:, :, 512 * int(slab[2]):512 * int(slab[2]) + 512]
        R.load(sp, K.banks1, slab, K.slab(R.slot(slab)), src)

    load("a0")
    load("g0")
    sp.dma_start(K.wf[:, :].rearrange("p (k r) -> p k r", k=DT), w_in[:, :, O_F:O_F + RANK]).then_inc(S("params_in"), 16)
    for slab in SLABS1[2:]:
        load(slab)


def load_params(K, eng):
    S, d = K.sem, K.d
    eng.dma_start(K.vec[:, :], d["vecs"]).then_inc(S("params_in"), 16)
    eng.dma_start(K.con[:, :], d["consts"]).then_inc(S("params_in"), 16)
    eng.dma_start(K.rowbuf[32:33, 0:NROW], d["rows"]).then_inc(S("params_in"), 16)
    eng.dma_start(K.w_gate_up(), d["w_gate_up"]).then_inc(S("params_in"), 16)




SETS = [("w1", 0), ("w1", 1), ("w3", 0), ("w3", 1), ("w2", 0), ("w2", 1)]
RSETS = 3
MOE_BANK = dict(pick=(0, 1), turn_sel=2, up=(3, 4), turn_h=5, down=(6, 7), put=(0, 1, 3, 4))


def moe_views(K):
    class V:
        x = K.tiles(0, DT)
        x_rows = K.tiles(1, TT, D)
        total = K.tiles(2, DT)
        picked = K.tiles(3, DT, P)
        sel = K.tiles(3, TT, P, 1024)
        wsel = K.tiles(3, TT, P, 1280)
        wsel_t = K.A(3, T, 1536)
        hidden = K.A(4, DE)
        hidden_t = K.tiles(4, ET, P, DE)
        y = K.A(4, D, 1024)
        w_router = K.tiles(5, DT, NG + NE)
        place = K.tiles(5, TT, NE, 576)
        weight = K.tiles(5, TT, NE, 704)
        chosen = K.tiles(5, TT, NE, 832)
    return V


def moe_set(K, i, k):
    at = (len(SLABS1) + 2 * (i % RSETS)) % RING * SLOT_COLS
    return K.ring[:, at:at + 2 * SLOT_COLS].rearrange("p (e k n) -> p e k n", e=QUAD, k=k)


def moe_pe(K, pe):
    S, ps, B = K.sem, K.psum, K.banks1
    V = moe_views(K)
    pe.wait_ge(S("x1"), DT)
    pe.wait_ge(S("router_in"), 16)
    for t in range(TT):
        pe_group(K, pe, B, f"logits{t}", [V.x[:, k, t * P:(t + 1) * P] for k in range(DT)],
                 [V.w_router[:, k, :] for k in range(DT)], out=(slice(0, P), slice(0, NG + NE)), bias=K.row("b_rt"))
    for t in range(TT):
        for half in range(2):
            b = B.take(pe, f"turn_x{t}_{half}")
            for j in range(4):
                m = pe.transpose(ps[:, b, j * P:(j + 1) * P], V.x[:, 4 * half + j, t * P:(t + 1) * P], K.c("ident"))
            m.then_inc(B.full[b], 1)
    pe.wait_ge(S("chosen"), 1)
    pe_group(K, pe, B, "before0", [K.c("before")], [V.chosen[:, 0, :]], out=(slice(0, P), slice(0, NE)))
    pe_group(K, pe, B, "before1", [K.c("ones"), K.c("before")], [V.chosen[:, 0, :], V.chosen[:, 1, :]],
             out=(slice(0, P), slice(0, NE)))
    pe_group(K, pe, B, "chose", [K.c("ones"), K.c("ones")], [V.chosen[:, 0, :], V.chosen[:, 1, :]],
             out=(slice(0, P), slice(0, NE)))
    pe.wait_ge(S("mem_squares"), 1)
    pe_group(K, pe, B, "mem_ms", [K.c("j1024")] * DT, [K.tiles(7, DT)[:, j, :] for j in range(DT)])
    pe.wait_ge(S("rounds_known"), 1)
    rounds = pe.value_load(K.rounds_int[0:1, 0:1], min_val=1, max_val=ROUNDS)
    with pe.Fori(0, rounds) as r:
        with pe.Fori(0, NQ) as q:
            n = r * NQ + q
            pe.wait_ge(S("sel_built"), n * 4 + 4)
            bank = MOE_BANK["turn_sel"]
            for t in range(TT):
                m = pe.transpose(ps[:, bank, t * P:(t + 1) * P], V.wsel[:, t, :], K.c("ident"))
            m.then_inc(S("sel_turned"), 1)
            pe.wait_ge(S("total_added"), n * 4 + 1)
            for half in range(2):
                bank = MOE_BANK["pick"][half]
                for j in range(4):
                    k = 4 * half + j
                    for t in range(TT):
                        m = pe.matmul(ps[:, bank, j * P:(j + 1) * P], V.x_rows[:, t, k::DT],
                                      V.sel[:, t, :], start=(t == 0), stop=(t == TT - 1))
                m.then_inc(S("picked"), 1)
            pe.wait_ge(S("picked_dve"), n + 1)
            pe.wait_ge(S("picked_act"), n + 1)
            for w, bank in enumerate(MOE_BANK["up"]):
                for half in range(2):
                    i = 2 * w + half
                    pe.wait_ge(S(f"moe_landed{i % RSETS}"), n * 32 + 16 * (i // RSETS + 1))
                    part = moe_set(K, i, DT // 2)
                    for j in range(DT // 2):
                        k = DT // 2 * half + j
                        for e in range(QUAD):
                            slots = slice(e * SLOTS, (e + 1) * SLOTS)
                            m = pe.matmul(ps[slots, bank, :], V.picked[:, k, slots], part[:, e, j, :],
                                          start=(k == 0), stop=(k == DT - 1))
                    m.then_inc(S(f"moe_read{i % RSETS}"), 1)
            pe.wait_ge(S("gated"), n + 1)
            for f in range(ET):
                m = pe.transpose(ps[:, MOE_BANK["turn_h"], f * P:(f + 1) * P], V.hidden[:, f::ET],
                                 K.c("ident"))
            m.then_inc(S("h_turned"), 1)
            pe.wait_ge(S("h_saved"), n + 1)
            for half in range(2):
                i = 4 + half
                pe.wait_ge(S(f"moe_landed{i % RSETS}"), n * 32 + 16 * (i // RSETS + 1))
                part = moe_set(K, i, ET // 2)
                for j in range(ET // 2):
                    f = ET // 2 * half + j
                    for c, bank in enumerate(MOE_BANK["down"]):
                        for e in range(QUAD):
                            slots = slice(e * SLOTS, (e + 1) * SLOTS)
                            m = pe.matmul(ps[slots, bank, :], V.hidden_t[:, f, slots],
                                          part[:, e, j, c * 512:(c + 1) * 512], start=(f == 0), stop=(f == ET - 1))
                m.then_inc(S(f"moe_read{i % RSETS}"), 1)
            pe.wait_ge(S("sel_saved"), n + 1)
            pe.wait_ge(S("y_dve"), n + 1)
            pe.wait_ge(S("y_act"), n + 1)
            for j, bank in enumerate(MOE_BANK["put"]):
                for half in range(2):
                    k = 2 * j + half
                    m = pe.matmul(ps[:, bank, half * T:(half + 1) * T], V.y[:, k * P:(k + 1) * P], V.wsel_t,
                                  start=True, stop=True)
                m.then_inc(S("put"), 1)
    pe.drain().then_inc(S("moe_over"), 1)
    x, sq = K.tiles(1, DT), K.tiles(3, DT)
    pe.wait_ge(S("pre_ln2"), 1)
    pe_group(K, pe, B, "ln2_mean", [K.c("j1024")] * DT, [x[:, j, :] for j in range(DT)])
    pe.wait_ge(S("ln2_squares"), 1)
    pe_group(K, pe, B, "ln2_var", [K.c("j1024")] * DT, [sq[:, j, :] for j in range(DT)])


def moe_act(K, act):
    S, ps, B, L = K.sem, K.psum, K.banks1, K.line("act", act)
    V = moe_views(K)
    W = router_views(K)
    for t in range(TT):
        b = B.wait_full(act, f"logits{t}")
        L.read(act.activation(W.logits[:, t, :], ps[:, b, 0:NG + NE], ACT.Copy), B, f"logits{t}")
    for t in range(TT):
        for half in range(2):
            g = f"turn_x{t}_{half}"
            b = B.wait_full(act, g)
            L.read(act.activation(V.x_rows[:, t, 512 * half:512 * half + 512], ps[:, b, :], ACT.Copy), B, g)
    act.wait_ge(S("group_below"), 1)
    L.done(act.activation(W.gexp, W.gexp, ACT.Exp), S("group_exp"))
    act.wait_ge(S("second_below"), 1)
    L.done(act.activation(W.e2, W.e2, ACT.Exp), S("second_exp"))
    act.wait_ge(S("second_in"), 32)
    L.done(act.activation(K.A(7), K.A(10), ACT.Square), S("mem_squares"))
    act_std(K, L, B, "mem_ms", K.A(8, T), "rms_eps")
    act.wait_ge(S("rounds_known"), 1)
    rounds = act.value_load(K.rounds_int[0:1, 0:1], min_val=1, max_val=ROUNDS)
    with act.Fori(0, rounds) as r:
        with act.Fori(0, NQ) as q:
            n = r * NQ + q
            act.wait_ge(S("sel_turned"), n + 1)
            act.activation(V.wsel_t, ps[:, MOE_BANK["turn_sel"], 0:T], ACT.Copy).then_inc(S("sel_saved"), 1)
            act.wait_ge(S("picked"), n * 2 + 2)
            act.activation(K.A(3, 512, 512), ps[:, MOE_BANK["pick"][1], :], ACT.Copy).then_inc(S("picked_act"), 1)
            act.wait_ge(S("moe_read1"), n * 2 + 2)
            act.activation(V.hidden, ps[:, MOE_BANK["up"][0], :], ACT.Silu).then_inc(S("silu"), 1)
            act.wait_ge(S("h_turned"), n + 1)
            act.activation(K.A(4, DE, DE), ps[:, MOE_BANK["turn_h"], :], ACT.Copy).then_inc(S("h_saved"), 1)
            act.wait_ge(S("moe_read2"), n * 2 + 3)
            act.activation(K.A(4, 512, 1536), ps[:, MOE_BANK["down"][1], :], ACT.Copy).then_inc(S("y_act"), 1)
    act.wait_ge(S("ln2_centred"), 1)
    L.done(act.activation(K.A(3), K.A(1), ACT.Square), S("ln2_squares"))
    act_std(K, L, B, "ln2_var", K.A(4, T), "ln_eps")


def router_views(K):
    class W:
        logits = K.tiles(6, TT, NG + NE)
        gmax = K.A(6, TT, 144)
        gexp = K.tiles(6, TT, NG, 146)
        gsum = K.A(6, TT, 162)
        eq8 = K.tiles(6, TT, NG, 164)
        oh8 = K.tiles(6, TT, NG, 180)
        best = K.A(6, TT, 196)
        masked = K.tiles(6, TT, NE, 198)
        eq = K.tiles(6, TT, NE, 326)
        oh1 = K.tiles(6, TT, NE, 454)
        oh2 = K.tiles(6, TT, NE, 582)
        m1 = K.A(6, TT, 710)
        m2 = K.A(6, TT, 712)
        e2 = K.A(6, TT, 714)
        w1 = K.A(6, TT, 716)
        w2 = K.A(6, TT, 718)
        most = K.A(6, 1, 720)
        over = K.A(6, ROUNDS, 722)
        count = K.A(6, 1, 730)
        chose = K.A(6, NE, 732)
    return W


def last(ap, n):
    p, a = ap.shape
    return ap.unsqueeze(2).to_broadcast([p, a, n])


def moe_dve(K, dve):
    S, ps, B, L = K.sem, K.psum, K.banks1, K.line("dve", dve)
    V, W = moe_views(K), router_views(K)
    step = S("router_steps")
    tt = lambda out, a, b, op: L.done(dve.tensor_tensor(out, a, b, op), step)
    ts = lambda out, a, s1, s2, op0, op1=None: L.done(
        dve.tensor_scalar(out, a, s1, s2, op0, op1) if op1 is not None else dve.tensor_scalar(out, a, s1, None, op0), step)
    peak = lambda out, a, op=ALU.max: L.done(dve.tensor_reduce(out, a, AX, op), step)

    def first_max(out, values, scratch, rank, n):
        peak(W.best, values)
        tt(scratch, values, last(W.best, n), ALU.is_equal)
        tt(scratch, scratch, wide(rank, TT), ALU.mult)
        peak(W.gsum, scratch)
        tt(out, scratch, last(W.gsum, n), ALU.is_equal)

    for t in range(TT):
        B.wait_read(dve, f"logits{t}")
    glog = W.logits[:, :, 0:NG]
    first_max(W.oh8, glog, W.eq8, K.c("rank8"), NG)
    tt(W.gexp, glog, last(W.best, NG), ALU.subtract)
    dve.sem_inc(S("group_below"), 1)
    ts(W.eq8, W.oh8, -1.0, BIG, ALU.add, ALU.mult)
    for t in range(TT):
        tt(W.masked[:, t, :].rearrange("p (g e) -> p g e", g=NG),
           W.logits[:, t, NG:].rearrange("p (g e) -> p g e", g=NG), last(W.eq8[:, t, :], EPG), ALU.add)
    first_max(W.oh1, W.masked, W.eq, K.c("rank64"), NE)
    L.done(dve.tensor_copy(W.m1, W.best), step)
    L.done(dve.scalar_tensor_tensor(K.A(6, TT * NE, 198), K.A(6, TT * NE, 454), -4.0 * BIG, K.A(6, TT * NE, 198),
                                    ALU.mult, ALU.add), step)
    first_max(W.oh2, W.masked, W.eq, K.c("rank64"), NE)
    tt(W.e2, W.best, W.m1, ALU.subtract)
    dve.sem_inc(S("second_below"), 1)
    tt(V.chosen, W.oh1, W.oh2, ALU.add)
    dve.sem_inc(S("chosen"), 1)
    dve.wait_ge(S("group_exp"), 1)
    peak(W.gsum, W.gexp, ALU.add)
    L.done(dve.reciprocal(W.gsum, W.gsum), step)
    dve.wait_ge(S("second_exp"), 1)
    ts(W.w1, W.e2, 1.0, None, ALU.add)
    L.done(dve.reciprocal(W.w1, W.w1), step)
    tt(W.w1, W.w1, W.gsum, ALU.mult)
    tt(W.w2, W.w1, W.e2, ALU.mult)
    tt(W.oh1, W.oh1, last(W.w1, NE), ALU.mult)
    tt(W.oh2, W.oh2, last(W.w2, NE), ALU.mult)
    tt(V.weight, W.oh1, W.oh2, ALU.add)
    for t in range(TT):
        b = B.wait_full(dve, f"before{t}")
        L.read(dve.scalar_tensor_tensor(V.place[:, t, :], ps[:, b, 0:NE], 1.0, V.chosen[:, t, :], ALU.add, ALU.mult),
               B, f"before{t}")
    ts(V.place, V.place, -1.0, None, ALU.add)
    b = B.wait_full(dve, "chose")
    L.read(dve.tensor_reduce(W.most, ps[:, b, 0:NE], AX, ALU.max), B, "chose")
    ts(W.over, K.c("rounds"), W.most, None, ALU.is_lt)
    peak(W.count, W.over, ALU.add)
    L.done(dve.tensor_copy(K.rounds_int[:, :], W.count), S("rounds_cast"))
    dve.sem_inc(S("rounds_known"), 1)
    L.done(dve.memset(K.A(2), 0.0), S("total_added"))
    for t in range(TT):
        for half in range(2):
            B.wait_read(dve, f"turn_x{t}_{half}")

    rounds = dve.value_load(K.rounds_int[0:1, 0:1], min_val=1, max_val=ROUNDS)
    by_slot = lambda ap: ap.rearrange("p (e s) -> p e s", e=QUAD)
    with dve.Fori(0, rounds) as r:
        with dve.Fori(0, NQ) as q:
            n = r * NQ + q
            for t in range(TT):
                dve.tensor_tensor(by_slot(V.sel[:, t, :]), wide(K.c("slot_iota"), QUAD),
                                  last(V.place[:, t, bass.ds(q * QUAD, QUAD)], SLOTS), ALU.is_equal)                   .then_inc(S("sel_built"), 1)
            dve.wait_ge(S("sel_built"), n * 4 + 2)
            for t in range(TT):
                dve.tensor_tensor(by_slot(V.wsel[:, t, :]), by_slot(V.sel[:, t, :]),
                                  last(V.weight[:, t, bass.ds(q * QUAD, QUAD)], SLOTS), ALU.mult)                   .then_inc(S("sel_built"), 1)
            dve.wait_ge(S("picked"), n * 2 + 1)
            dve.tensor_copy(K.A(3, 512), ps[:, MOE_BANK["pick"][0], :]).then_inc(S("picked_dve"), 1)
            dve.wait_ge(S("silu"), n + 1)
            dve.wait_ge(S("moe_read0"), n * 2 + 3)
            dve.tensor_tensor(V.hidden, V.hidden, ps[:, MOE_BANK["up"][1], :], ALU.mult).then_inc(S("gated"), 1)
            dve.wait_ge(S("moe_read2"), n * 2 + 3)
            dve.tensor_copy(K.A(4, 512, 1024), ps[:, MOE_BANK["down"][0], :]).then_inc(S("y_dve"), 1)
            for j, bank in enumerate(MOE_BANK["put"]):
                dve.wait_ge(S("put"), n * 4 + j + 1)
                part = K.A(2, 512, 512 * j)
                dve.tensor_tensor(part, part, ps[:, bank, :], ALU.add).then_inc(S("total_added"), 1)
            dve.wait_ge(S("total_added"), n * 4 + 5)
        ins = dve.tensor_scalar(K.A(5, TT * NE, 576), K.A(5, TT * NE, 576), -float(SLOTS), None, ALU.add)
        ins.then_inc(S("round_moved"), 1)
        dve.wait_ge(S("round_moved"), r + 1)
    one = S("ln2_steps")
    L.done(dve.scalar_tensor_tensor(K.A(1), K.A(0), ALPHA1, K.A(2), ALU.mult, ALU.add), S("pre_ln2"))
    dve.wait_ge(S("second_in"), 32)
    dve_rstd(K, L, B, "mem_ms", K.A(8, T))
    mem = K.tiles(10, DT)
    for m in range(DT):
        L.done(dve.scalar_tensor_tensor(mem[:, m, :], mem[:, m, :], K.v("n_mem", m), K.A(8, T), ALU.mult, ALU.mult),
               S("mem_normed"))
    x = K.tiles(1, DT)
    b = B.wait_full(dve, "ln2_mean")
    L.read(dve.tensor_tensor(x, x, wide(ps[:, b, 0:T], DT), ALU.subtract), B, "ln2_mean")
    dve.sem_inc(S("ln2_centred"), 1)
    dve_rstd(K, L, B, "ln2_var", K.A(4, T))
    L.done(dve.tensor_tensor(x, x, wide(K.A(4, T), DT), ALU.mult), one)
    for m in range(DT):
        L.done(dve.tensor_scalar(K.tiles(0, DT)[:, m, :], x[:, m, :], K.v("ln2_g", m), K.v("ln2_b", m),
                                 ALU.mult, ALU.add), S("x2"))


def moe_sp(K, sp):
    S, d = K.sem, K.d
    w = {name: d[name].rearrange("e (p h k) n -> h p e (k n)", p=P, h=2) for name in ("w1", "w3", "w2")}

    def load(i, first, wait):
        name, half = SETS[i]
        sp.wait_ge(S(f"moe_read{i % RSETS}"), wait)
        sp.sem_inc(S("set_wanted"), 1)
        sp.dma_start(moe_set(K, i, 1).rearrange("p e k n -> p e (k n)"), w[name][half, :, bass.ds(first, QUAD), :])\
          .then_inc(S(f"moe_landed{i % RSETS}"), 16)

    for i in range(RSETS):
        load(i, 0, 1)
    sp.wait_ge(S("rounds_known"), 1)
    rounds = sp.value_load(K.rounds_int[0:1, 0:1], min_val=1, max_val=ROUNDS)
    with sp.Fori(0, rounds * NQ - 1) as n:
        for i in range(RSETS, 2 * RSETS):
            load(i, (n & (NQ - 1)) * QUAD, n * 2 + 2)
        for i in range(RSETS):
            load(i, ((n + 1) & (NQ - 1)) * QUAD, n * 2 + 3)
    for i in range(RSETS, 2 * RSETS):
        load(i, (NQ - 1) * QUAD, (rounds * NQ - 1) * 2 + 2)


GATES = 16
LEVEL_ORDER = [6, 0, 1, 2, 3, 4, 5]


class Views2:
    def __init__(self, K):
        half = lambda s, h: K.tiles(s, HH, T, 1024 * h)
        pair = lambda s, q: K.tiles(s, 2, T, 512 * q)
        self.h, self.u = K.tiles(0, DT), K.tiles(1, DT)
        self.qf, self.key = half(2, 0), half(2, 1)
        self.b, self.logf = half(3, 0), half(3, 1)
        self.decay, self.qd = half(4, 0), half(4, 1)
        self.kd, self.att = half(5, 0), half(5, 1)
        self.prob = [pair(12, i) for i in range(4)]
        self.prob_t = [pair(13, i) for i in range(4)]
        self.hi, self.hg, self.pz, self.sq = (pair(6, i) for i in range(4))
        self.sk = K.A(7, T)
        self.sv = K.tiles(7, TT, ADH, 256)
        self.iq = K.tiles(7, 4, T, 384)
        self.ik = K.A(7, T, 1408)
        self.iw = K.tiles(7, TT, IH, 1664)
        self.rstd = K.A(7, T, 1680)
        self.stat = lambda a, n: K.A(7, n, 1936 + a)
        self.mq, self.mk, self.mv, self.ya = (pair(8, i) for i in range(4))
        self.gate = [K.A(14 + i // DT, T, T * (i % DT)) for i in range(GATES)]
        self.yb, self.yc, self.ym, self.relu1 = (pair(9, i) for i in range(4))
        self.mem = K.tiles(10, DT)
        self.score, self.work, self.not_kept, self.relu2 = (pair(10, i) for i in range(4))
        self.kdec = K.A(10, 1024).rearrange("p (t h k) -> p t h k", t=TT, h=HH)
        self.state = K.A(5, 3 * HH * HDV).rearrange("p (c h v) -> p c h v", c=3, h=HH)
        self.merged = K.rowbuf[:, :].rearrange("p (k t) -> p k t", k=DT)
        self.pool_w = K.wf[:, :].rearrange("p (g d) -> p g d", g=2)


def second_pe(K, pe):
    B, R, S, ps = K.banks2, K.ring2, K.sem, K.psum
    V = Views2(K)
    names = lambda n, a, c: [f"{n}{m}" for m in range(a, a + c)]
    x = V.u

    def norm(group, wait, squares):
        pe.wait_ge(S(wait), 1)
        pe_group(K, pe, B, group, [K.c("j1024")] * DT, [squares[:, j, :] for j in range(DT)])

    pe.wait_ge(S("mem_normed"), DT)
    w = K.slab(R.wait_landed(pe, "mem"))
    for m in range(2):
        pe_group(K, pe, B, f"mk{m}", [w[:, k, m * P:(m + 1) * P] for k in range(DT)], [V.mem[:, k, :] for k in range(DT)])
    for t in range(TT):
        pe_group(K, pe, B, f"mv{t}", [V.mem[:, k, t * P:(t + 1) * P] for k in range(DT)],
                 [w[:, k, 256:512] for k in range(DT)])
    R.last_group["mem"] = "mv1"
    norm("pre_ms", "pre_squares", K.tiles(3, DT))
    pe.wait_ge(S("u"), DT)
    pe_slab_tiles(K, pe, B, R, "z0", names("hq", 0, 4), x)
    pe_slab_tiles(K, pe, B, R, "z1", names("hf", 0, 4), x)

    def rows(w, name, c, n):
        for t in range(TT):
            pe_group(K, pe, B, f"{name}{t}", [x[:, k, t * P:(t + 1) * P] for k in range(DT)],
                     [w[:, k, c:c + n] for k in range(DT)], out=(slice(0, P), slice(0, n)))

    def doubled(w, name, c):
        b = B.take(pe, name)
        for half in range(2):
            for k in range(DT):
                m = pe.matmul(ps[64 * half:64 * half + 64, b, 0:T], w[:, k, c:c + 64], x[:, k, :],
                              start=(k == 0), stop=(k == DT - 1))
        m.then_inc(B.full[b], 1)

    def level(i):
        n = LEVEL_ORDER[i]
        pe.wait_ge(S("decayed"), 2 * i + 2)
        q, k = (V.qd, V.kd) if n < LEVELS - 1 else (V.qf, V.key)
        for t in range(TT):
            b = B.take(pe, f"level{n}_{t}")
            for h in range(HH):
                m = pe.matmul(ps[:, b, h * P:(h + 1) * P], k[:, h, t * P:(t + 1) * P], q[:, h, t * P:(t + 1) * P],
                              start=True, stop=True)
            m.then_inc(B.full[b], 1)

    def scores(name, h, q, keys):
        r = slice(64 * (h % 2), 64 * (h % 2) + 64)
        b = B.take(pe, f"{name}{h}")
        for t in range(TT):
            m = pe.matmul(ps[:, b, t * T:(t + 1) * T], q[r, h // 2, t * P:(t + 1) * P], keys(h, r), start=True, stop=True)
        m.then_inc(B.full[b], 1)

    def turn_probs(name, h):
        pe.wait_ge(S(f"{name}_done"), h + 1)
        b = B.take(pe, f"{name}_t{h}")
        for s in range(TT):
            for t in range(TT):
                m = pe.transpose(ps[:, b, (s * TT + t) * P:(s * TT + t + 1) * P],
                                 V.prob[h][:, t, s * P:(s + 1) * P], K.c("ident"))
        m.then_inc(B.full[b], 1)

    def values(name, h, v):
        r = slice(64 * (h % 2), 64 * (h % 2) + 64)
        B.wait_read(pe, f"{name}_t{h}")
        pe_group(K, pe, B, f"{name}_o{h}", [v(h, s) for s in range(TT)], [V.prob_t[h][:, s, :] for s in range(TT)],
                 out=(r, slice(0, T)))

    def gates(i, half):
        pe_slab_tiles(K, pe, B, R, f"gate{i}_{half}", names(f"gate{i}_", 4 * half, 4), x)

    def branch(i, y, slab, place):
        w = K.slab(R.wait_landed(pe, slab), 4)
        for m in range(DT):
            pe_group(K, pe, B, f"br{i}_{m}", [w[:, 2 * place + k, m * P:(m + 1) * P] for k in range(2)],
                     [y[:, k, :] for k in range(2)])
        R.last_group[slab] = f"br{i}_{DT - 1}"

    level(0)
    pe_slab_tiles(K, pe, B, R, "z2", names("hg", 0, 2), x, first=2, last=False)
    rows(K.slab(R.slot("z2")), "hi", 0, 256)
    R.last_group["z2"] = "hi1"
    level(1)
    pe_slab_tiles(K, pe, B, R, "z3", names("pz", 0, 2) + names("sq", 0, 2), x)
    level(2)
    pe_slab_tiles(K, pe, B, R, "z4", names("iq", 0, 3), x, first=1, last=False)
    w = K.slab(R.slot("z4"))
    doubled(w, "sk", 0)
    rows(w, "sv", 64, 64)
    R.last_group["z4"] = "sv1"
    level(3)
    pe_slab_tiles(K, pe, B, R, "z5", ["iq3"], x, last=False)
    w = K.slab(R.slot("z5"))
    doubled(w, "ik", 128)
    rows(w, "iw", 192, 8)
    for m in range(2):
        pe_group(K, pe, B, f"mq{m}", [w[:, k, 200 + m * P:200 + (m + 1) * P] for k in range(DT)],
                 [x[:, k, :] for k in range(DT)])
    R.last_group["z5"] = "mq1"
    level(4)
    gates(1, 0)
    level(5)
    gates(1, 1)
    level(6)
    gates(3, 0)
    pe.wait_ge(S("keys_end"), 1)
    for t in range(TT):
        b = B.take(pe, f"keys_t{t}")
        for h in range(HH):
            m = pe.transpose(ps[:, b, h * P:(h + 1) * P], V.kd[:, h, t * P:(t + 1) * P], K.c("ident"))
        m.then_inc(B.full[b], 1)
    pe.wait_ge(S("pooled"), 4)
    pe.wait_ge(S("pool_w_in"), 16)
    for g in range(4):
        r = slice(64 * (g % 2), 64 * (g % 2) + 64)
        pe_group(K, pe, B, f"pool{g}", [V.pool_w[r, g // 2, :]], [V.pz[r, g // 2, :]], out=(r, slice(0, T)))
    for t in range(TT):
        B.wait_read(pe, f"keys_t{t}")
        B.wait_read(pe, f"hi{t}")
    for c in range(NC - 1):
        t, r = c // 2, slice(CHUNK * (c % 2), CHUNK * (c % 2) + CHUNK)
        b = B.take(pe, f"hkv{c}")
        for h in range(HH):
            m = pe.matmul(ps[:, b, h * HDV:(h + 1) * HDV], V.kdec[r, t, h, :], V.hi[r, t, h * HDV:(h + 1) * HDV],
                          start=True, stop=True)
        m.then_inc(B.full[b], 1)
    for g in ("iq0", "iq1", "iq2", "iq3", "ik"):
        B.wait_read(pe, g)
    for h in range(IH):
        scores("is", h, V.iq, lambda h, r: V.ik[r, :])
    gates(3, 1)
    for g in ("mk0", "mk1", "mq0", "mq1"):
        B.wait_read(pe, g)
    for h in range(AH):
        scores("ms", h, V.mq, lambda h, r: V.mk[r, h // 2, :])
    pe.wait_ge(S("att_done"), 1)
    pe.wait_ge(S("hstate"), NC - 1)
    att = K.A(5, 1024, 1024).rearrange("p (t h s) -> p t h s", t=TT, h=HH)
    for h in range(HH):
        r = slice(64 * (h % 2), 64 * (h % 2) + 64)
        b = B.take(pe, f"ho{h}")
        for t in range(TT):
            pe.matmul(ps[r, b, t * P:(t + 1) * P], V.hi[:, t, h * HDV:(h + 1) * HDV], att[:, t, h, :],
                      start=True, stop=False)
            for c in (2 * t, 2 * t + 1):
                if c:
                    m = pe.matmul(ps[r, b, c * CHUNK:(c + 1) * CHUNK], V.state[:, c - 1, h, :],
                                  V.qd[:, h, c * CHUNK:(c + 1) * CHUNK], start=False, stop=(c % 2 == 1))
        m.then_inc(B.full[b], 1)
    for g in range(4):
        B.wait_read(pe, f"pool{g}")
    branch(1, V.yb, "br13", 0)
    for h in range(AH):
        turn_probs("ms", h)
    for t in range(TT):
        B.wait_read(pe, f"mv{t}")
    for h in range(AH):
        values("ms", h, lambda h, s: V.mv[:, s, h * 64:(h + 1) * 64])
    pe.wait_ge(S("ho_squares"), 1)
    for m in range(2):
        pe_group(K, pe, B, f"ho_ms{m}", [K.c("j64")], [V.relu1[:, m, :]])
    gates(0, 0)
    for h in range(AH):
        B.wait_read(pe, f"ms_o{h}")
    branch(3, V.ym, "br13", 1)
    gates(0, 1)
    for g in ("sq0", "sq1", "sk", "sv0", "sv1"):
        B.wait_read(pe, g)
    for h in range(AH):
        scores("ss", h, V.sq, lambda h, r: V.sk[r, :])
    pe.wait_ge(S("ya"), 2)
    branch(0, V.ya, "br02", 0)
    gates(2, 0)
    for h in range(AH):
        turn_probs("ss", h)
    for h in range(AH):
        values("ss", h, lambda h, s: V.sv[:, s, :])
    gates(2, 1)
    for h in range(AH):
        B.wait_read(pe, f"ss_o{h}")
    branch(2, V.yc, "br02", 1)

    pe.wait_ge(S("merged"), 4 * DT)
    for s in range(2):
        pe_slab_tiles(K, pe, B, R, f"o{s}", names("oz", 4 * s, 4), V.merged)
    norm("post_ms", "post_squares", K.tiles(3, DT))
    norm("ffn_ms", "ffn_squares", K.tiles(3, DT))
    pe.wait_ge(S("u2"), DT)
    for i in range(11):
        pe_slab_tiles(K, pe, B, R, f"ff{i}", names("ff", 4 * i, 4), x)
    hidden = K.arena[:, 2 * 2048:2 * 2048 + FT * T].rearrange("p (f t) -> p f t", f=FT)
    down = [B.take(pe, f"dn{m}") for m in range(DT)]
    for i in range(6):
        w = K.slab(R.wait_landed(pe, f"dn{i}"), 4)
        for j in range(min(4, FT - 4 * i)):
            f = 4 * i + j
            pe.wait_ge(S("hidden"), f + 1)
            for m in range(DT):
                ins = pe.matmul(ps[:, down[m], 0:T], w[:, j, m * P:(m + 1) * P], hidden[:, f, :],
                                start=(f == 0), stop=(f == FT - 1))
                if f == FT - 1:
                    ins.then_inc(B.full[down[m]], 1)
                elif j == 3 and m == DT - 1:
                    ins.then_inc(S("down_read"), 1)
    norm("last_ms", "last_squares", K.tiles(3, DT))


def second_act(K, act):
    B, S, ps, L = K.banks2, K.sem, K.psum, K.line("act", act)
    V = Views2(K)

    def evac(group, out, func=ACT.Copy, bias=0.0, scale=1.0, rows=slice(0, P), cols=slice(0, T), sem=None):
        b = B.wait_full(act, group)
        L.read(act.activation(out, ps[rows, b, cols], func, bias=bias, scale=scale), B, group)

    def squares(out, src, sem):
        L.done(act.activation(out, src, ACT.Square), S(sem))

    act.wait_ge(S("second_in"), 32)
    act.wait_ge(S("x2"), DT)
    for m in range(2):
        evac(f"mk{m}", V.mk[:, m, :])
    for t in range(TT):
        evac(f"mv{t}", V.mv[:, t, :])
    squares(K.A(3), K.A(0), "pre_squares")
    act_std(K, L, B, "pre_ms", V.rstd, "rms_eps")
    act.wait_ge(S("lb_below"), 1)
    L.done(act.activation(V.stat(0, HH), V.stat(0, HH), ACT.Exp), S("lb_exp"))
    for h in range(HH):
        evac(f"hq{h}", V.qf[:, h, :], ACT.Silu)
    for h in range(HH):
        evac(f"hf{h}", V.logf[:, h, :], ACT.Sigmoid)
    act.wait_ge(S("forget"), 1)
    L.done(act.activation(K.A(3, 1024, 1024), K.A(3, 1024, 1024), ACT.Ln), S("log_forget"))

    def level_exp(n):
        act.wait_ge(S("level_below"), n + 1)
        L.done(act.activation(K.A(4, 1024), K.A(4, 1024), ACT.Exp), S("level_exp"))

    level_exp(0)
    for m in range(2):
        evac(f"hg{m}", V.hg[:, m, :], ACT.Silu)
    for t in range(TT):
        evac(f"hi{t}", V.hi[:, t, :])
    level_exp(1)
    for m in range(2):
        evac(f"pz{m}", V.pz[:, m, :])
    for m in range(2):
        evac(f"sq{m}", V.sq[:, m, :], scale=ADH ** -0.5)
    level_exp(2)
    for m in range(3):
        evac(f"iq{m}", V.iq[:, m, :])
    evac("sk", V.sk)
    for t in range(TT):
        evac(f"sv{t}", V.sv[:, t, :], cols=slice(0, ADH))
    level_exp(3)
    evac("iq3", V.iq[:, 3, :])
    evac("ik", V.ik)
    for t in range(TT):
        evac(f"iw{t}", V.iw[:, t, :], scale=IH ** -0.5, cols=slice(0, IH))
    for m in range(2):
        evac(f"mq{m}", V.mq[:, m, :], scale=ADH ** -0.5)

    def exps(name):
        for h in range(AH):
            act.wait_ge(S(f"{name}_below"), h + 1)
            L.done(act.activation(V.prob[h], V.prob[h], ACT.Exp), S(f"{name}_exp"))

    def probs_and_out(name, y):
        for h in range(AH):
            evac(f"{name}_t{h}", V.prob_t[h], cols=slice(0, 512))
        for h in range(AH):
            r = slice(64 * (h % 2), 64 * (h % 2) + 64)
            evac(f"{name}_o{h}", y[r, h // 2, :], rows=r)

    seen = [0]

    def gates(i, half):
        for m in range(4 * half, 4 * half + 4):
            n = seen[0]
            seen[0] += 1
            if n >= GATES:
                act.wait_ge(S("merged"), n - GATES + 1)
            evac(f"gate{i}_{m}", V.gate[n % GATES], ACT.Sigmoid)

    level_exp(4)
    gates(1, 0)
    level_exp(5)
    gates(1, 1)
    act.wait_ge(S("end_below"), 1)
    L.done(act.activation(K.A(4, 1024), K.A(4, 1024), ACT.Exp), S("end_exp"))
    act.wait_ge(S("keys_end"), 1)
    L.done(act.activation(K.A(4, 1024), K.A(3, 1024), ACT.Exp), S("start_exp"))
    gates(3, 0)
    for t in range(TT):
        evac(f"keys_t{t}", K.A(10, 512, 512 * t), cols=slice(0, 512))
    for g in range(4):
        r = slice(64 * (g % 2), 64 * (g % 2) + 64)
        evac(f"pool{g}", V.yb[r, g // 2, :], scale=K.vec[r, VEC["pool_s"][0] + g // 2:VEC["pool_s"][0] + g // 2 + 1],
             rows=r)
    for h in range(IH):
        if h >= 2:
            act.wait_ge(S("indexed"), TT * (h - 1))
        evac(f"is{h}", V.relu1 if h % 2 else V.relu2, ACT.Relu, scale=IDX_SCALE, cols=slice(0, 512))
    gates(3, 1)
    exps("ms")
    for h in range(HH):
        r = slice(64 * (h % 2), 64 * (h % 2) + 64)
        evac(f"ho{h}", V.ya[r, h // 2, :], rows=r)
    squares(K.A(9, 512, 1536), K.A(8, 512, 1536), "ho_squares")
    probs_and_out("ms", V.ym)
    for m in range(2):
        act_std(K, L, B, f"ho_ms{m}", V.relu2[:, m, :], "rms_eps")
    gates(0, 0)
    gates(0, 1)
    exps("ss")
    gates(2, 0)
    probs_and_out("ss", V.yc)
    gates(2, 1)
    for m in range(DT):
        evac(f"oz{m}", K.tiles(2, DT)[:, m, :])
    squares(K.A(3), K.A(2), "post_squares")
    act_std(K, L, B, "post_ms", V.rstd, "rms_eps")
    act.wait_ge(S("h2"), 1)
    squares(K.A(3), K.A(0), "ffn_squares")
    act_std(K, L, B, "ffn_ms", V.rstd, "rms_eps")
    hidden = K.arena[:, 2 * 2048:2 * 2048 + FT * T].rearrange("p (f t) -> p f t", f=FT)
    for f in range(FT):
        evac(f"ff{f}", hidden[:, f, :], ACT.Silu)
    for m in range(DT):
        evac(f"dn{m}", V.u[:, m, :])
    squares(K.A(3), K.A(1), "last_squares")
    act_std(K, L, B, "last_ms", V.rstd, "rms_eps")


IDX_SCALE = 64 ** -0.5


def second_dve(K, dve):
    B, S, ps, L = K.banks2, K.sem, K.psum, K.line("dve", dve)
    V = Views2(K)
    step = S("second_steps")
    tt = lambda out, a, b, op, sem=step: L.done(dve.tensor_tensor(out, a, b, op), sem)
    ts = lambda out, a, s1, s2, op0, op1, sem=step: L.done(dve.tensor_scalar(out, a, s1, s2, op0, op1), sem)
    stt = lambda out, a, s, b, op0, op1, sem=step: L.done(dve.scalar_tensor_tensor(out, a, s, b, op0, op1), sem)
    peak = lambda out, a, op=ALU.max: L.done(dve.tensor_reduce(out, a, AX, op), step)

    dve.wait_ge(S("second_in"), 32)
    dve_rstd(K, L, B, "pre_ms", V.rstd)
    for m in range(DT):
        stt(V.u[:, m, :], V.h[:, m, :], K.v("n_mix_pre", m), V.rstd, ALU.mult, ALU.mult, S("u"))

    lb, keep = V.stat(0, HH), V.stat(HH, HH)
    lbl = K.v("lb", 0, HH)
    tt(lb, lbl, lbl, ALU.max)
    tt(lb, lbl, lb, ALU.subtract)
    dve.sem_inc(S("lb_below"), 1)
    dve.wait_ge(S("lb_exp"), 1)
    L.done(dve.reciprocal(keep, lb), step)
    tt(lb, lb, keep, ALU.mult)
    tt(lb, lb, lb, ALU.subtract)
    ts(keep, lb, -1.0, 1.0, ALU.mult, ALU.add)
    for h in range(HH):
        B.wait_read(dve, f"hf{h}")
        sg = V.logf[:, h, :]
        ts(V.key[:, h, :], sg, -1.0, 1.0, ALU.mult, ALU.add)
        ts(V.key[:, h, :], V.key[:, h, :], keep[:, h:h + 1], None, ALU.mult, ALU.bypass)
        ts(sg, sg, keep[:, h:h + 1], lb[:, h:h + 1], ALU.mult, ALU.add)
    ts(K.A(3, 1024, 1024), K.A(3, 1024, 1024), 1e-30, None, ALU.max, ALU.bypass)
    dve.sem_inc(S("forget"), 1)
    for h in range(HH):
        B.wait_read(dve, f"hq{h}")
    dve.sem_inc(S("decayed"), 2)

    def softmax(name, masked):
        mx = V.stat(8, 2 * AH)
        for h in range(AH):
            b = B.wait_full(dve, f"{name}{h}")
            s = ps[:, b, :].rearrange("p (t k) -> p t k", t=TT)
            m = mx[:, 2 * h:2 * h + 2]
            if masked:
                L.read(dve.tensor_tensor(V.prob[h], s, V.not_kept, ALU.add), B, f"{name}{h}")
                peak(m, V.prob[h])
                tt(V.prob[h], V.prob[h], last(m, T), ALU.subtract)
            else:
                peak(m, s)
                L.read(dve.tensor_tensor(V.prob[h], s, last(m, T), ALU.subtract), B, f"{name}{h}")
            dve.sem_inc(S(f"{name}_below"), 1)
        for h in range(AH):
            m = mx[:, 2 * h:2 * h + 2]
            dve.wait_ge(S(f"{name}_exp"), h + 1)
            peak(m, V.prob[h], ALU.add)
            L.done(dve.reciprocal(m, m), step)
            tt(V.prob[h], V.prob[h], last(m, T), ALU.mult, S(f"{name}_done"))

    count = [0]

    def merge(i):
        for m in range(DT):
            gate = V.gate[count[0] % GATES]
            B.wait_read(dve, f"gate{i}_{m}")
            b = B.wait_full(dve, f"br{i}_{m}")
            out = V.merged[:, m, :] if count[0] < DT else gate
            L.read(dve.tensor_tensor(out, ps[:, b, 0:T], gate, ALU.mult), B, f"br{i}_{m}")
            if count[0] >= DT:
                tt(V.merged[:, m, :], V.merged[:, m, :], gate, ALU.add, S("merged_more"))
            dve.sem_inc(S("merged"), 1)
            count[0] += 1

    def pooling():
        for m in range(2):
            B.wait_read(dve, f"pz{m}")
        z, win, inv = V.pz, [V.relu1, V.yc], K.c2("inv_count").rearrange("p (g t) -> p g t", g=2)
        src = z
        for i, w in enumerate((1, 2, 4, 8)):
            dst = win[i % 2]
            L.done(dve.tensor_copy(dst[:, :, 0:w], src[:, :, 0:w]), step)
            tt(dst[:, :, w:T], src[:, :, w:T], src[:, :, 0:T - w], ALU.add)
            r = slice(64 * (i % 2), 64 * (i % 2) + 64)
            g = i // 2
            out = V.ya[r, g, :]
            tt(out, dst[r, g, :], inv[r, g, :], ALU.mult)
            src = dst
        for g in range(4):
            r = slice(64 * (g % 2), 64 * (g % 2) + 64)
            tt(z[r, g // 2, :], V.ya[r, g // 2, :], z[r, g // 2, :], ALU.subtract, S("pooled"))

    def indexer():
        for t in range(TT):
            B.wait_read(dve, f"iw{t}")
        for h in range(IH):
            B.wait_read(dve, f"is{h}")
            relu = V.relu1 if h % 2 else V.relu2
            for t in range(TT):
                before = K.c2("not_adm").rearrange("p (t k) -> p t k", t=TT) if h == 0 else V.score
                stt(V.score[:, t, :], relu[:, t, :], V.iw[:, t, h:h + 1], before[:, t, :], ALU.mult, ALU.add, S("indexed"))

    def keep_largest():
        top = V.stat(16, 8)
        for t in range(TT):
            for i in range(NSEL // 8):
                src = V.score if i == 0 else V.work
                L.done(dve.max(top, src[:, t, :]), step)
                L.done(dve.match_replace(V.work[:, t, :], top, src[:, t, :], -3e38), step)
        tt(V.not_kept, V.work, V.score, ALU.is_lt)
        flat = lambda i: K.A(10, 512, 512 * i)
        stt(flat(2), flat(0), -0.5 * BIG, flat(2), ALU.is_gt, ALU.mult)
        ts(flat(2), flat(2), -1.0, BIG, ALU.add, ALU.mult)
        dve.sem_inc(S("kept"), 1)

    dve.wait_ge(S("log_forget"), 1)
    L.done(dve.memset(K.A(4, 1024), 1.0), step)
    L.done(dve.memset(K.A(4, 1024).rearrange("p (c s) -> p c s", s=CHUNK)[:, :, 0:1], 0.0), step)
    L.done(dve.tensor_tensor_scan(K.A(3, 1024), K.A(4, 1024), K.A(3, 1024, 1024), 0.0, ALU.mult, ALU.add), step)
    b_all, d_all = K.A(3, 1024), K.A(4, 1024)
    att = K.A(5, 1024, 1024)

    def decay_level(n):
        half = 32 >> n
        v = lambda a: a.rearrange("p (c s) -> p c s", s=2 * half)
        mid = v(b_all)[:, :, half - 1:half].to_broadcast([P, 1024 // (2 * half), 2 * half])
        tt(v(d_all), v(b_all), mid, ALU.subtract)
        stt(d_all, d_all, -1.0, d_all, ALU.mult, ALU.min)
        dve.sem_inc(S("level_below"), 1)
        dve.wait_ge(S("level_exp"), n + 1)
        dve.tensor_tensor(K.A(4, 1024, 1024), K.A(2, 1024), d_all, ALU.mult).then_inc(S("decayed"), 1)
        dve.tensor_tensor(K.A(5, 1024), K.A(2, 1024, 1024), d_all, ALU.mult).then_inc(S("decayed"), 1)
        dve.wait_ge(S("decayed"), 2 * n + 4)

    def add_level(n):
        mask = K.c2("level")[:, n * P:(n + 1) * P]
        for t in range(TT):
            g = f"level{n}_{t}"
            b = B.wait_full(dve, g)
            part = att[:, 512 * t:512 * t + 512]
            out = part if n == LEVEL_ORDER[0] else K.A(10, 512)
            heads = lambda a: a.rearrange("p (h s) -> p h s", h=HH)
            L.read(dve.tensor_tensor(heads(out), heads(ps[:, b, :]), wide(mask, HH), ALU.mult), B, g)
            if n != LEVEL_ORDER[0]:
                tt(part, part, out, ALU.add)

    decay_level(0)
    add_level(LEVELS - 1)
    for n in range(LEVELS - 1):
        add_level(n)
        if n < LEVELS - 2:
            decay_level(n + 1)
    dve.sem_inc(S("att_done"), 1)
    v = lambda a: a.rearrange("p (c s) -> p c s", s=CHUNK)
    end = v(b_all)[:, :, CHUNK - 1:CHUNK]
    tt(v(d_all), end.to_broadcast([P, HH * NC, CHUNK]), v(b_all), ALU.subtract)
    dve.sem_inc(S("end_below"), 1)
    dve.wait_ge(S("end_exp"), 1)
    tt(K.A(5, 1024), K.A(2, 1024, 1024), d_all, ALU.mult)
    dve.sem_inc(S("keys_end"), 1)
    dve.wait_ge(S("start_exp"), 1)
    tt(K.A(4, 1024, 1024), K.A(2, 1024), d_all, ALU.mult)
    pooling()
    whole = d_all.rearrange("p (h c s) -> p h c s", h=HH, c=NC)
    for c in range(NC - 1):
        b = B.wait_full(dve, f"hkv{c}")
        for h in range(HH):
            kv = ps[:, b, h * HDV:(h + 1) * HDV]
            out = V.state[:, c, h, :]
            if c == 0:
                ins = dve.tensor_copy(out, kv)
            else:
                ins = dve.scalar_tensor_tensor(out, V.state[:, c - 1, h, :], whole[:, h, c, CHUNK - 1:CHUNK], kv,
                                               ALU.mult, ALU.add)
            if h == HH - 1:
                L.read(ins, B, f"hkv{c}")
            else:
                L.done(ins, step)
        dve.sem_inc(S("hstate"), 1)
    indexer()
    softmax("ms", False)
    merge(1)
    for m in range(2):
        r = V.relu2[:, m, :]
        dve_rstd(K, L, B, f"ho_ms{m}", r)
        stt(r, r, K.v("hg_g", m), V.hg[:, m, :], ALU.mult, ALU.mult)
        tt(V.ya[:, m, :], V.ya[:, m, :], r, ALU.mult, S("ya"))
    keep_largest()
    merge(3)
    softmax("ss", True)
    merge(0)
    merge(2)

    def add_normed(z, group, gain):
        dve_rstd(K, L, B, group, V.rstd)
        for m in range(DT):
            stt(z[:, m, :], z[:, m, :], K.v(gain, m), V.rstd, ALU.mult, ALU.mult)

    add_normed(K.tiles(2, DT), "post_ms", "n_mix_post")
    tt(K.A(0), K.A(0), K.A(2), ALU.add)
    dve.sem_inc(S("h2"), 1)
    dve_rstd(K, L, B, "ffn_ms", V.rstd)
    for m in range(DT):
        stt(V.u[:, m, :], V.h[:, m, :], K.v("n_ffn_pre", m), V.rstd, ALU.mult, ALU.mult, S("u2"))
    hidden = K.arena[:, 2 * 2048:2 * 2048 + FT * T].rearrange("p (f t) -> p f t", f=FT)
    for f in range(FT):
        g = f"ff{FT + f}"
        b = B.wait_full(dve, g)
        B.wait_read(dve, f"ff{f}")
        L.read(dve.tensor_tensor(hidden[:, f, :], hidden[:, f, :], ps[:, b, 0:T], ALU.mult), B, g)
        dve.sem_inc(S("hidden"), 1)
    add_normed(V.u, "last_ms", "n_ffn_post")
    tt(K.A(0), K.A(0), K.A(1), ALU.add)
    dve.sem_inc(S("out"), 1)


def second_sp(K, sp):
    S, R, B, d = K.sem, K.ring2, K.banks2, K.d
    by_tile = lambda w: w.rearrange("(k p) n -> p k n", p=P)
    sp.wait_ge(S("moe_over"), 1)

    def load(slab, src, k=DT):
        view = K.slab(R.slot(slab), k)
        R.load(sp, B, slab, view[:, 0:src.shape[1], 0:src.shape[2]], src)

    load("mem", by_tile(d["w_mem_kv_2"]))
    for i in range(6):
        load(f"z{i}", by_tile(d["w_in_2"])[:, :, 512 * i:min(512 * i + 512, N_IN2)])
        if i == 0:
            sp.dma_start(Views2(K).pool_w, d["pool_w_2"].rearrange("(a b) c d -> (b c) a d", b=2)).then_inc(S("pool_w_in"), 16)

    def gates(i):
        for s in range(2):
            load(f"gate{i}_{s}", by_tile(d["w_gate_2"][i])[:, :, 512 * s:512 * s + 512])

    def branches(first):
        src = d["w_branch_2"].rearrange("(a b) (k p) n -> b p a k n", b=2, p=P)[first]
        slab = f"br{first}{first + 2}"
        R.wait_free(sp, B, slab)
        view = K.slab(R.slot(slab), 4)
        for a in range(2):
            sp.dma_start(view[:, 2 * a:2 * a + 2, :], src[:, a]).then_inc(R.landed[R.slot(slab)], 16)

    gates(1)
    gates(3)
    branches(1)
    gates(0)
    branches(0)
    gates(2)
    for s in range(2):
        load(f"o{s}", by_tile(d["w_out_2"])[:, :, 512 * s:512 * s + 512])
    for i in range(11):
        load(f"ff{i}", by_tile(d["w_ffn_gate_up_2"])[:, :, 512 * i:512 * i + 512])
    for i in range(6):
        src, slot = by_tile(d["w_ffn_down_2"])[:, 4 * i:min(4 * i + 4, FT), :], R.slot(f"dn{i}")
        if i < RING2:
            R.wait_free(sp, B, f"dn{i}")
        else:
            sp.wait_ge(S("down_read"), i - RING2 + 1)
        sp.dma_start(K.slab(slot, 4)[:, 0:src.shape[1], :], src).then_inc(R.landed[slot], 16)


def host_arrays(inputs):
    a = {n: np.asarray(v) for n, v in inputs.items()}
    col = lambda v: np.ascontiguousarray(v).reshape(-1, P).T
    b = a["b_in"][0]
    f = np.zeros((P,), np.float32)
    f[:RANK] = b[O_F:O_F + RANK]
    packed = dict(b_a=col(b[O_A:O_A + D]), b_g=col(b[O_G:O_G + D]), b_q=col(b[O_Q:O_Q + GDK]),
                  b_r=col(b[O_R:O_R + D]), b_f=f[:, None], b_ga=col(b[O_GA:O_GA + D]), b_gb=col(b[O_GB:O_GB + D]),
                  conv_w=a["conv_w"][0].reshape(CW, DT, P).transpose(2, 1, 0).reshape(P, DT * CW),
                  conv_b=col(a["conv_b"]), cln_g=col(a["conv_ln_g"]), cln_b=col(a["conv_ln_b"]),
                  b_co=col(a["b_conv_out"]), gla_g=col(a["gla_norm_g"]), b_out=col(a["b_out"]),
                  ln1_g=col(a["ln1_g"]), ln1_b=col(a["ln1_b"]), ln2_g=col(a["ln2_g"]), ln2_b=col(a["ln2_b"]),
                  lb=col(a["lb_logits_2"]), hg_g=col(a["hgrn_norm_2"]), pool_s=col(a["pool_scale_2"]),
                  n_mem=col(a["norm_mem_2"]), n_mix_pre=col(a["norm_mix_pre_2"]),
                  n_mix_post=col(a["norm_mix_post_2"]), n_ffn_pre=col(a["norm_ffn_pre_2"]),
                  n_ffn_post=col(a["norm_ffn_post_2"]))
    assert all(packed[n].shape[1] == m for n, m in VEC_SIZES.items())
    con, con2 = constants()
    out = {
        "x": np.ascontiguousarray(a["x"][0].T), "mem": np.ascontiguousarray(a["mem_2"][0].T),
        "vecs": np.ascontiguousarray(np.concatenate([packed[n] for n in VEC_SIZES], 1)),
        "rows": np.concatenate([b[O_K:O_K + GDK], b[O_V:O_V + GDV],
                                a["b_router_group"][0], a["b_router_expert"][0]])[None, :],
        "w_gate_up": np.concatenate([a["w_gate_up"][0], a["b_gate_up"]], 0),
        "w_router": np.concatenate([a["w_router_group"][0], a["w_router_expert"][0]], 1),
        "consts": con, "consts2": con2,
    }
    for n in ("w_in", "w_conv_out", "w_gla_out", "w_out", "w1", "w3", "w2", "w_in_2", "w_gate_2",
              "w_branch_2", "w_out_2", "pool_w_2", "w_mem_kv_2", "w_ffn_gate_up_2", "w_ffn_down_2"):
        out[n] = a[n][0]
    return {n: np.ascontiguousarray(v) for n, v in out.items()}


INPUTS = ("x", "mem", "vecs", "rows", "consts", "consts2", "w_router", "w_in", "w_conv_out", "w_gate_up", "w_gla_out",
          "w_out", "w1", "w3", "w2", "w_in_2", "w_gate_2", "w_branch_2", "w_out_2", "pool_w_2", "w_mem_kv_2",
          "w_ffn_gate_up_2", "w_ffn_down_2")


def two_blocks(nc, d, out):
    with ExitStack() as ctx:
        K = Chip(nc, ctx, d)
        block = ctx.enter_context(nc.Block())

        @block.tensor
        def _(pe):
            block1_pe(K, pe)
            moe_pe(K, pe)
            second_pe(K, pe)

        @block.scalar
        def _(act):
            load_params(K, act)
            block1_act(K, act)
            moe_act(K, act)
            second_act(K, act)

        @block.vector
        def _(dve):
            block1_dve(K, dve)
            moe_dve(K, dve)
            second_dve(K, dve)

        @block.sync
        def _(sp):
            block1_sp(K, sp)
            sp.wait_ge(K.sem("pre_ln1"), 1)
            sp.dma_start(moe_views(K).w_router, d["w_router"].rearrange("(k p) n -> p k n", p=P))\
              .then_inc(K.sem("router_in"), 16)
            sp.dma_start(K.A(11, NCON2), d["consts2"]).then_inc(K.sem("second_in"), 16)
            sp.dma_start(K.tiles(10, DT), d["mem"].rearrange("(k p) t -> p k t", p=P)).then_inc(K.sem("second_in"), 16)
            moe_sp(K, sp)
            second_sp(K, sp)
            sp.wait_ge(K.sem("out"), 1)
            sp.dma_start(out.rearrange("(k p) t -> p k t", p=P), K.tiles(0, DT)).then_inc(K.sem("stored"), 16)
            sp.wait_ge(K.sem("stored"), 16)


def kernel(**inputs):
    import concourse.bacc as bacc
    from concourse.bass_utils import run_bass_kernel_spmd

    arrays = host_arrays(inputs)
    arrays = {f"in_{n}": arrays[n] for n in INPUTS}
    nc = bacc.Bacc("TRN2", target_bir_lowering=False, num_devices=1)
    d = {n: nc.dram_tensor(f"in_{n}", arrays[f"in_{n}"].shape, F32, kind="ExternalInput").ap() for n in INPUTS}
    out = nc.dram_tensor("out_0", (D, T), F32, kind="ExternalOutput").ap()
    two_blocks(nc, d, out)
    r = run_bass_kernel_spmd(nc, [arrays], core_ids=[0])
    return np.ascontiguousarray(r.results[0]["out_0"].T)[None]
```

```python
from contextlib import ExitStack

import numpy as np

import concourse.bass as bass
from concourse import mybir

F32 = mybir.dt.float32
F32R = mybir.dt.float32r
I32 = mybir.dt.int32
ALU = mybir.AluOpType
ACT = mybir.ActivationFunctionType
AX = mybir.AxisListType.X

P = 128
T = 256
TT = T // P
D = 1024
DT = D // P
CHUNK = 64
NC = T // CHUNK
CW = 31
PAD = CW - 1
GH = 4
GDK, GDV, RANK = 512, 1024, 16
NG, EPG, NE = 8, 8, 64
DE = 512
ET = DE // P
SLOTS = 32
QUAD = 4
NQ = NE // QUAD
ROUNDS = T // SLOTS
HH, HDV = 4, 64
AH, ADH = 4, 64
IH = 8
FF = 2816
FT = FF // P
NSEL = 64
SLOT_COLS = 4096
RING = 6
RING2 = 4
RING2_FIRST = 2
SHARED_COLS = 8 * 2048 + (RING - RING2) * SLOT_COLS
LN_EPS, RMS_EPS = 1e-5, 1e-6
ALPHA1 = 2.0 ** 0.25
BIG = 1e30

O_A, O_G, O_Q, O_K, O_V, O_R, O_F = 0, 1024, 2048, 2560, 3072, 4096, 5120
O_GA, O_GB = 5136, 6160
Z_HQ, Z_HF, Z_HI, Z_PZ, Z_SK, Z_IQ3 = 0, 512, 1024, 1536, 2048, 2560
N_IN2 = 3016

VEC_SIZES = dict(b_a=8, b_g=8, b_q=4, b_r=8, b_f=1, b_ga=8, b_gb=8, conv_w=8 * CW, conv_b=8, cln_g=8,
                 cln_b=8, b_co=8, gla_g=8, b_out=8, ln1_g=8, ln1_b=8, ln2_g=8, ln2_b=8, lb=4,
                 hg_g=2, pool_s=2, n_mem=8, n_mix_pre=8, n_mix_post=8, n_ffn_pre=8, n_ffn_post=8)
ROW_SIZES = dict(b_k=512, b_v=1024, b_rt=NG + NE)
CONST_SIZES = dict(ident=P, after=P, before=P, ones=P, j1024=P, j256=P, j64=P, chunk_of=2,
                   slot_iota=SLOTS, ln_eps=1, rms_eps=1, rounds=ROUNDS, rank8=NG, rank64=NE)
CONST2_SIZES = dict(level=7 * P, inv_count=2 * T, not_adm=TT * T)
LEVELS = 7


def columns(sizes):
    at, out = 0, {}
    for name, n in sizes.items():
        out[name] = (at, n)
        at += n
    return out, at


VEC, NVEC = columns(VEC_SIZES)
ROW, NROW = columns(ROW_SIZES)
CON, NCON = columns(CONST_SIZES)
CON2, NCON2 = columns(CONST2_SIZES)


def constants():
    i = np.arange(P)
    s, t = i[:, None], i[None, :]
    c = np.zeros((P, NCON), np.float32)
    put = lambda n, v: c.__setitem__((slice(None), slice(CON[n][0], sum(CON[n]))), v)
    put("ident", s == t)
    put("after", (s > t) & (s // CHUNK == t // CHUNK))
    put("before", s < t)
    put("ones", 1.0)
    put("j1024", 1.0 / D)
    put("j256", 1.0 / T)
    put("j64", (s // HDV == t // HDV) / HDV)
    put("chunk_of", s // CHUNK == np.arange(2)[None, :])
    put("slot_iota", np.arange(SLOTS)[None, :])
    put("rounds", SLOTS * np.arange(ROUNDS)[None, :])
    put("ln_eps", LN_EPS)
    put("rms_eps", RMS_EPS)
    put("rank8", NG - np.arange(NG)[None, :])
    put("rank64", NE - np.arange(NE)[None, :])
    d = np.zeros((P, NCON2), np.float32)
    for n in range(LEVELS - 1):
        h = 32 >> n
        m = (s // (2 * h) == t // (2 * h)) & (s % (2 * h) < h) & (t % (2 * h) >= h)
        d[:, n * P:(n + 1) * P] = m
    d[:, 6 * P:7 * P] = s == t
    for g, w in enumerate((2, 4, 8, 16)):
        a = CON2["inv_count"][0] + T * (g // 2)
        d[64 * (g % 2):64 * (g % 2) + 64, a:a + T] = 1.0 / np.minimum(np.arange(T) + 1, w)
    for tile in range(TT):
        q = tile * P + i
        a = CON2["not_adm"][0] + T * tile
        d[:, a:a + T] = np.where(np.arange(T)[None, :] < ((q // CHUNK + 1) * CHUNK)[:, None], 0.0, -BIG)
    return c, d


class Banks:

    def __init__(self, sem, name):
        self.full = [sem(f"{name}_full{b}") for b in range(8)]
        self.free = [sem(f"{name}_free{b}") for b in range(8)]
        self.uses, self.place, self.turn = [0] * 8, {}, 0

    def take(self, pe, group):
        b = self.turn % 8
        self.turn += 1
        if self.uses[b]:
            pe.wait_ge(self.free[b], self.uses[b])
        self.uses[b] += 1
        self.place[group] = (b, self.uses[b])
        return b

    def wait_full(self, eng, group):
        b, n = self.place[group]
        eng.wait_ge(self.full[b], n)
        return b

    def wait_read(self, eng, group):
        b, n = self.place[group]
        eng.wait_ge(self.free[b], n)

    def free_of(self, group):
        return self.free[self.place[group][0]]


class Ring:

    def __init__(self, sem, name, slabs, slots, first=0):
        self.slots, self.first = slots, first
        self.landed = [sem(f"{name}_landed{s}") for s in range(slots)]
        self.slabs, self.last_group = slabs, {}
        self.index = {s: i for i, s in enumerate(slabs)}
        self.count = {}
        for i, s in enumerate(slabs):
            before = self.count[slabs[i - slots]] if i >= slots else 0
            self.count[s] = before + 16 * (2 if s.startswith("br") else 0 if s == "a0" else 1)

    def wait_landed(self, pe, slab):
        pe.wait_ge(self.landed[self.slot(slab)], self.count[slab])
        return self.slot(slab)

    def slot(self, slab):
        return (self.first + self.index[slab]) % self.slots

    def load(self, sp, banks, slab, dst, src):
        self.wait_free(sp, banks, slab)
        sp.dma_start(dst, src).then_inc(self.landed[self.slot(slab)], 16)

    def wait_free(self, sp, banks, slab):
        i = self.index[slab]
        if i >= self.slots:
            banks.wait_full(sp, self.last_group[self.slabs[i - self.slots]])


class Line:

    def __init__(self, eng):
        self.eng, self.count = eng, {}

    def done(self, ins, sem):
        ins.then_inc(sem, 1)
        self.count[sem.name] = self.count.get(sem.name, 0) + 1
        self.eng.wait_ge(sem, self.count[sem.name])

    def read(self, ins, banks, group):
        ins.then_inc(banks.free_of(group), 1)
        banks.wait_read(self.eng, group)


SLABS1 = ["a0", "g0", "a1", "g1", "k", "q", "v0", "v1", "r0", "r1", "ga0", "ga1", "gb0", "gb1",
          "co0", "co1", "go0", "go1", "wo0", "wo1"]
SLABS2 = (["mem", "z0", "z1", "z2", "z3", "z4", "z5", "gate1_0", "gate1_1", "gate3_0", "gate3_1", "br13",
           "gate0_0", "gate0_1", "gate2_0", "br02", "gate2_1", "o0", "o1"]
          + [f"ff{i}" for i in range(11)] + [f"dn{i}" for i in range(6)])
IN_COLS = dict(a0=O_A, a1=O_A + 512, g0=O_G, g1=O_G + 512, k=O_K, q=O_Q, v0=O_V, v1=O_V + 512,
               r0=O_R, r1=O_R + 512, ga0=O_GA, ga1=O_GA + 512, gb0=O_GB, gb1=O_GB + 512)


class Chip:

    def __init__(self, nc, ctx, d):
        self.nc, self.ctx, self.d = nc, ctx, d
        self.names, self.lines = {}, {}
        sb = lambda name, cols, dt=F32: ctx.enter_context(nc.sbuf_tensor(name, [P, cols], dt))
        with nc.sbuf_tensor("shared", [P, SHARED_COLS], F32) as self.shared:
            pass
        self.parts_of = sb("parts", SHARED_COLS, F32R)
        self.ring = sb("ring", RING2 * SLOT_COLS)
        self.arena = sb("arena", 4 * 2048)
        self.con = sb("con", NCON)
        self.vec = sb("vec", NVEC)
        self.wf = sb("wf", DT * RANK)
        self.small = sb("small", GH * NC)
        self.rowbuf = sb("rowbuf", DT * T)
        self.rounds_int = sb("rounds_int", 1, I32)
        self.psum = ctx.enter_context(nc.psum_tensor("psum", [P, 8, 512], F32))
        self.banks1 = self.banks2 = Banks(self.sem, "bank")
        self.ring1 = Ring(self.sem, "ring1", SLABS1, RING)
        self.ring2 = Ring(self.sem, "ring2", SLABS2, RING2, first=RING2_FIRST)

    def sem(self, name):
        if name not in self.names:
            self.names[name] = self.ctx.enter_context(self.nc.semaphore(name))
        return self.names[name]

    def line(self, name, eng):
        return self.lines.setdefault(name, Line(eng))

    def A(self, slot, cols=2048, at=0):
        if slot >= 4:
            a = (slot - 4) * 2048 + at
            return self.shared[:, a:a + cols]
        return self.arena[:, slot * 2048 + at:slot * 2048 + at + cols]

    def parts(self, slot, cols=2048, at=0):
        a = (slot - 4) * 2048 + at
        return self.parts_of[:, a:a + cols]

    def ring_cols(self, at, cols):
        if at >= RING2 * SLOT_COLS:
            a = at - RING2 * SLOT_COLS + 8 * 2048
            return self.shared[:, a:a + cols]
        return self.ring[:, at:at + cols]

    def tiles(self, slot, n, w=T, at=0):
        return self.A(slot, n * w, at).rearrange("p (k t) -> p k t", k=n)

    def c(self, name):
        a, n = CON[name]
        return self.con[:, a:a + n]

    def c2(self, name):
        a, n = CON2[name]
        return self.A(11, n, a)

    def v(self, name, i=0, n=1):
        a = VEC[name][0] + i
        return self.vec[:, a:a + n]

    def row(self, name, at=0, n=None):
        a, m = ROW[name]
        return self.rowbuf[32:33, a + at:a + at + (m if n is None else n)]

    def w_gate_up(self):
        return self.rowbuf[0:RANK + 1, 0:GDK]

    def f_low(self, rows=RANK):
        return self.rowbuf[0:rows, GDK:GDK + T]

    def chunk_decay(self):
        return self.small[:, 0:GH * NC]

    def rstd(self, i):
        return self.A(2, T, 1024 if i == 3 else 240 + T * i)

    def slab(self, slot, k=DT):
        return self.ring_cols(slot * SLOT_COLS, SLOT_COLS).rearrange("p (k n) -> p k n", k=k)



def pe_group(K, pe, banks, group, weights, acts, out=(slice(0, P), slice(0, T)), bias=None):
    b = banks.take(pe, group)
    o = K.psum[out[0], b, out[1]]
    n = len(weights)
    for k in range(n):
        m = pe.matmul(o, weights[k], acts[k], start=(k == 0), stop=(k == n - 1 and bias is None))
    if bias is not None:
        m = pe.matmul(o, K.con[32:33, CON["ones"][0]:CON["ones"][0] + P], bias, start=False, stop=True)
    m.then_inc(banks.full[b], 1)


def pe_slab_tiles(K, pe, banks, ring, slab, groups, acts, first=0, last=True):
    w = K.slab(ring.wait_landed(pe, slab))
    for m, group in enumerate(groups):
        c = (first + m) * P
        pe_group(K, pe, banks, group, [w[:, k, c:c + P] for k in range(DT)], [acts[:, k, :] for k in range(DT)])
    if last:
        ring.last_group[slab] = groups[-1]


def pe_mean_by_tile(K, pe, banks, group, x, sem):
    b = banks.take(pe, group)
    for j in range(DT):
        pe.wait_ge(K.sem(sem), j + 1)
        m = pe.matmul(K.psum[:, b, 0:T], K.c("j1024"), x[:, j, :], start=(j == 0), stop=(j == DT - 1))
    m.then_inc(banks.full[b], 1)


def act_squares(K, line, out, x, wanted, sem):
    for m in range(DT):
        line.eng.wait_ge(K.sem(wanted), m + 1)
        line.done(line.eng.activation(out[:, m, :], x[:, m, :], ACT.Square), K.sem(sem))


def act_affine(K, line, out, x, gain, shift, wanted, sem):
    for m in range(DT):
        line.eng.wait_ge(K.sem(wanted), m + 1)
        line.done(line.eng.activation(out[:, m, :], x[:, m, :], ACT.Identity, bias=K.v(shift, m), scale=K.v(gain, m)),
                  K.sem(sem))


def dve_centre(K, line, banks, group, x, sem):
    b = banks.wait_full(line.eng, group)
    for m in range(DT):
        ins = line.eng.tensor_tensor(x[:, m, :], x[:, m, :], K.psum[:, b, 0:T], ALU.subtract)
        if m < DT - 1:
            line.done(ins, K.sem(sem))
        else:
            line.read(ins, banks, group)
            line.eng.sem_inc(K.sem(sem), 1)


def act_std(K, line, banks, group, out, eps):
    b = banks.wait_full(line.eng, group)
    line.read(line.eng.activation(out, K.psum[:, b, 0:T], ACT.Sqrt, bias=K.c(eps)), banks, group)


def dve_rstd(K, line, banks, group, out):
    banks.wait_read(line.eng, group)
    line.done(line.eng.reciprocal(out, out), K.sem("reciprocals"))


def wide(ap, n):
    p, w = ap.shape
    return ap.unsqueeze(1).to_broadcast([p, n, w])



def upad(K):
    return K.arena[:, 2048:2048 + DT * (T + PAD)].rearrange("p (k t) -> p k t", k=DT)


def block1_pe(K, pe):
    B, R, S = K.banks1, K.ring1, K.sem
    x = K.tiles(0, DT)
    tiles = lambda name, a, n: [f"{name}{m}" for m in range(a, a + n)]
    q = K.tiles(5, GH)
    k = K.tiles(5, TT, GDK, GH * T)
    v = K.tiles(6, TT, GDV)
    la = K.tiles(10, TT, GDK)
    kdec = K.tiles(10, TT, GDK, TT * GDK)
    state = K.tiles(2, GH, 256, 1024)

    pe.wait_ge(S("x_in"), 16)
    w = K.slab(0)
    for m in range(4):
        pe.wait_ge(S(f"first_in{m}"), 16)
        pe_group(K, pe, B, f"a{m}", [w[:, j, m * P:(m + 1) * P] for j in range(DT)], [x[:, j, :] for j in range(DT)])
    R.last_group["a0"] = "a3"
    for slab, name, a in (("g0", "g", 0), ("a1", "a", 4), ("g1", "g", 4)):
        pe_slab_tiles(K, pe, B, R, slab, tiles(name, a, 4), x)
    pe.wait_ge(S("params_in"), 80)
    wf = K.wf[:, :].rearrange("p (k r) -> p k r", k=DT)
    pe_group(K, pe, B, "f", [wf[:, j, :] for j in range(DT)], [x[:, j, :] for j in range(DT)],
             out=(slice(0, RANK), slice(0, T)))

    def rows(slab, name, bias):
        w = K.slab(R.wait_landed(pe, slab))
        for t in range(TT):
            pe_group(K, pe, B, f"{name}_{t}", [x[:, j, t * P:(t + 1) * P] for j in range(DT)],
                     [w[:, j, :] for j in range(DT)], out=(slice(0, P), slice(0, 512)), bias=bias)
        R.last_group[slab] = f"{name}_{TT - 1}"

    row = K.row
    rows("k", "k", row("b_k"))
    pe_slab_tiles(K, pe, B, R, "q", tiles("q", 0, 4), x)
    B.wait_read(pe, "f")
    for t in range(TT):
        pe_group(K, pe, B, f"z_{t}", [K.f_low(RANK + 1)[:, t * P:(t + 1) * P]], [K.w_gate_up()],
                 out=(slice(0, P), slice(0, 512)))
    rows("v0", "v0", row("b_v", 0, 512))
    rows("v1", "v1", row("b_v", 512, 512))
    for slab, name, a in (("r0", "r", 0), ("r1", "r", 4), ("ga0", "ga", 0), ("ga1", "ga", 4)):
        pe_slab_tiles(K, pe, B, R, slab, tiles(name, a, 4), x)

    pe.wait_ge(S("log_decay"), TT)
    for t in range(TT):
        pe_group(K, pe, B, f"later_{t}", [K.c("after")], [la[:, t, :]], out=(slice(0, P), slice(0, 512)))
    b = B.take(pe, "chunk_sum")
    for h in range(GH):
        for t in range(TT):
            o = K.psum[:, b, h * NC + 2 * t:h * NC + 2 * t + 2]
            m = pe.matmul(o, la[:, t, h * P:(h + 1) * P], K.c("chunk_of"), start=True, stop=True)
    m.then_inc(B.full[b], 1)
    pe.wait_ge(S("conv_sum"), 1)
    conv, squares = K.tiles(3, DT), K.tiles(1, DT)
    pe_group(K, pe, B, "conv_mean", [K.c("j1024")] * DT, [conv[:, j, :] for j in range(DT)])
    pe_slab_tiles(K, pe, B, R, "gb0", tiles("gb", 0, 4), x)
    pe.wait_ge(S("conv_squares"), 1)
    pe_group(K, pe, B, "conv_var", [K.c("j1024")] * DT, [squares[:, j, :] for j in range(DT)])

    pe.wait_ge(S("keys_decayed"), 1)
    for c in range(NC):
        t, r = c // 2, slice(CHUNK * (c % 2), CHUNK * (c % 2) + CHUNK)
        for pair in range(2):
            b = B.take(pe, f"kv{c}_{pair}")
            for h in (2 * pair, 2 * pair + 1):
                m = pe.matmul(K.psum[:, b, 256 * (h % 2):256 * (h % 2) + 256], kdec[r, t, h * P:(h + 1) * P],
                              v[r, t, 256 * h:256 * h + 256], start=True, stop=True)
            m.then_inc(B.full[b], 1)
        pe_slab_tiles(K, pe, B, R, "gb1", [f"gb{4 + c}"], x, first=c)
        pe.wait_ge(S("state"), c + 1)
        b = B.take(pe, f"o{c}")
        for h in range(GH):
            for half in range(2):
                m = pe.matmul(K.psum[:, b, (2 * h + half) * CHUNK:(2 * h + half + 1) * CHUNK],
                              state[:, h, half * P:(half + 1) * P], q[:, h, c * CHUNK:(c + 1) * CHUNK],
                              start=True, stop=True)
        m.then_inc(B.full[b], 1)

    pe.wait_ge(S("conv_act"), DT)
    cu = K.tiles(4, DT)
    pe_slab_tiles(K, pe, B, R, "co0", tiles("co", 0, 4), cu)
    pe.wait_ge(S("o_squares"), 1)
    sq = K.tiles(10, DT)
    for h in range(GH):
        pe_group(K, pe, B, f"o_ms{h}", [K.c("j256")] * 2, [sq[:, 2 * h, :], sq[:, 2 * h + 1, :]])
    pe_slab_tiles(K, pe, B, R, "co1", tiles("co", 4, 4), cu)
    pe.drain().then_inc(S("moe_read0"), 1)
    pe.wait_ge(S("gla_in"), 1)
    y = K.tiles(7, DT)
    for s in range(2):
        pe_slab_tiles(K, pe, B, R, f"go{s}", tiles("go", 4 * s, 4), y)
    pe.drain().then_inc(S("moe_read1"), 1)
    m8 = K.tiles(8, DT)
    for s in range(2):
        w = K.slab(R.wait_landed(pe, f"wo{s}"))
        for m in range(4):
            b = B.take(pe, f"wo{4 * s + m}")
            for j in range(DT):
                if s == m == 0:
                    pe.wait_ge(S("merged1"), j + 1)
                ins = pe.matmul(K.psum[:, b, 0:T], w[:, j, m * P:(m + 1) * P], m8[:, j, :], start=(j == 0),
                                stop=(j == DT - 1))
            ins.then_inc(B.full[b], 1)
        R.last_group[f"wo{s}"] = f"wo{4 * s + 3}"
    pe.drain().then_inc(S("moe_read2"), 1)
    pe_mean_by_tile(K, pe, B, "ln1_mean", K.tiles(1, DT), "pre_ln1")
    pe_mean_by_tile(K, pe, B, "ln1_var", K.tiles(3, DT), "ln1_squares")


def block1_act(K, act):
    B, S, L = K.banks1, K.sem, K.line("act", act)
    ps = K.psum
    act.wait_ge(S("params_in"), 80)
    sg = K.tiles(4, DT)

    def evac(group, out, func, bias=0.0, scale=1.0, rows=slice(0, P), cols=slice(0, T)):
        b = B.wait_full(act, group)
        L.read(act.activation(out, ps[rows, b, cols], func, bias=bias, scale=scale), B, group)

    for s in range(2):
        for m in range(4 * s, 4 * s + 4):
            evac(f"g{m}", sg[:, m, :], ACT.Sigmoid, bias=K.v("b_g", m))
    act.wait_ge(S("ones_row"), 1)
    evac("f", K.f_low(), ACT.Identity, bias=K.vec[0:RANK, VEC["b_f"][0]:VEC["b_f"][0] + 1], rows=slice(0, RANK))
    k = K.tiles(5, TT, GDK, GH * T)
    v = K.tiles(6, TT, GDV)
    for t in range(TT):
        evac(f"k_{t}", k[:, t, :], ACT.Copy, cols=slice(0, 512))
    q = K.tiles(5, GH)
    for h in range(GH):
        evac(f"q{h}", q[:, h, :], ACT.Identity, bias=K.v("b_q", h))
    soft = K.tiles(10, TT, GDK)
    logit = K.tiles(10, TT, GDK, TT * GDK)
    for t in range(TT):
        evac(f"z_{t}", logit[:, t, :], ACT.Copy, cols=slice(0, 512))
        L.done(act.activation(soft[:, t, :], logit[:, t, :], ACT.Abs), S("soft_steps"))
        L.done(act.activation(soft[:, t, :], soft[:, t, :], ACT.Exp, scale=-1.0), S("soft_steps"))
        L.done(act.activation(soft[:, t, :], soft[:, t, :], ACT.Ln, bias=1.0), S("soft"))
    for n in range(2):
        for t in range(TT):
            evac(f"v{n}_{t}", v[:, t, 512 * n:512 * n + 512], ACT.Copy, cols=slice(0, 512))
    for m in range(DT):
        evac(f"r{m}", K.tiles(7, DT)[:, m, :], ACT.Silu, bias=K.v("b_r", m))
    for m in range(DT):
        evac(f"ga{m}", K.tiles(8, DT)[:, m, :], ACT.Sigmoid, bias=K.v("b_ga", m))
    kdec = K.tiles(10, TT, GDK, TT * GDK)
    for t in range(TT):
        evac(f"later_{t}", kdec[:, t, :], ACT.Exp, scale=1.0 / 16.0, cols=slice(0, 512))
    evac("chunk_sum", K.chunk_decay(), ACT.Exp, scale=1.0 / 16.0, cols=slice(0, GH * NC))
    act.wait_ge(S("conv_centred"), 1)
    L.done(act.activation(K.A(1), K.A(3), ACT.Square), S("conv_squares"))

    def gate_b(m):
        evac(f"gb{m}", K.tiles(9, DT)[:, m, :], ACT.Sigmoid, bias=K.v("b_gb", m))

    for m in range(4):
        gate_b(m)
    act_std(K, L, B, "conv_var", K.rstd(0), "ln_eps")
    o = K.tiles(11, DT)
    for c in range(NC):
        gate_b(4 + c)
        evac(f"o{c}", o[:, :, c * CHUNK:(c + 1) * CHUNK], ACT.Copy, cols=slice(0, 512))
        if c == 1:
            act.wait_ge(S("conv_normed"), 1)
            for m in range(DT):
                L.done(act.activation(K.tiles(4, DT)[:, m, :], K.tiles(3, DT)[:, m, :], ACT.Silu,
                                      bias=K.v("cln_b", m), scale=K.v("cln_g", m)), S("conv_act"))
    L.done(act.activation(K.A(10), K.A(11), ACT.Square), S("o_squares"))
    for h in range(GH):
        act_std(K, L, B, f"o_ms{h}", K.rstd(h), "rms_eps")
    h1 = K.tiles(1, DT)
    for m in range(DT):
        evac(f"wo{m}", h1[:, m, :], ACT.Identity, bias=K.v("b_out", m))
    act_squares(K, L, K.tiles(3, DT), h1, "ln1_centred", "ln1_squares")
    act_std(K, L, B, "ln1_var", K.rstd(0), "ln_eps")
    act_affine(K, L, K.tiles(0, DT), h1, "ln1_g", "ln1_b", "ln1_scaled", "x1")


def block1_dve(K, dve):
    B, S, L = K.banks1, K.sem, K.line("dve", dve)
    ps = K.psum
    u = upad(K)
    L.done(dve.memset(K.f_low(RANK + 1), 1.0), S("ones_row"))
    L.done(dve.memset(u[:, :, 0:PAD], 0.0), S("pad"))
    dve.wait_ge(S("params_in"), 80)
    sg = K.tiles(4, DT)
    for m in range(DT):
        b = B.wait_full(dve, f"a{m}")
        B.wait_read(dve, f"g{m}")
        L.read(dve.scalar_tensor_tensor(u[:, m, PAD:PAD + T], ps[:, b, 0:T], K.v("b_a", m), sg[:, m, :],
                                        ALU.add, ALU.mult), B, f"a{m}")
    conv = K.tiles(3, DT)
    cw = K.v("conv_w", 0, DT * CW).rearrange("p (k w) -> p k w", k=DT)
    taps = S("taps")
    for m in range(DT):
        dve.tensor_scalar(conv[:, m, :], u[:, m, 0:T], cw[:, m, 0:1], K.v("conv_b", m), ALU.mult, ALU.add)\
           .then_inc(taps, 1)
    with dve.Fori(1, CW) as w:
        for m in range(DT):
            dve.wait_ge(taps, (w - 1) * DT + m + 1)
            dve.scalar_tensor_tensor(conv[:, m, :], u[:, m, bass.ds(w, T)], cw[:, m, bass.ds(w, 1)], conv[:, m, :],
                                     ALU.mult, ALU.add).then_inc(taps, 1)
    dve.wait_ge(taps, CW * DT)
    dve.sem_inc(S("conv_sum"), 1)
    soft = K.tiles(10, TT, GDK)
    logit = K.tiles(10, TT, GDK, TT * GDK)
    dve.wait_ge(S("soft"), TT)
    for t in range(TT):
        L.done(dve.scalar_tensor_tensor(soft[:, t, :], logit[:, t, :], 0.0, soft[:, t, :], ALU.min, ALU.subtract),
               S("log_decay"))

    q = K.A(5, GH * T)
    for h in range(GH):
        B.wait_read(dve, f"q{h}")
    L.done(dve.tensor_scalar(q, q, float(P) ** -0.5, None, ALU.mult), S("q_scaled"))

    def centre(x, group, sem):
        b = B.wait_full(dve, group)
        L.read(dve.tensor_tensor(x, x, wide(ps[:, b, 0:T], DT), ALU.subtract), B, group)
        dve.sem_inc(sem, 1)

    centre(conv, "conv_mean", S("conv_centred"))
    kdec, k = K.A(10, 1024, 1024), K.A(5, 1024, GH * T)
    for t in range(TT):
        B.wait_read(dve, f"later_{t}")
        B.wait_read(dve, f"k_{t}")
    L.done(dve.tensor_tensor(kdec, kdec, k, ALU.mult), S("keys_decayed"))
    state = K.tiles(2, GH, 256, 1024)
    B.wait_read(dve, "chunk_sum")
    dec = K.chunk_decay().rearrange("p (h c) -> p h c", h=GH)
    for c in range(NC):
        for h in range(GH):
            g = f"kv{c}_{h // 2}"
            b = B.wait_full(dve, g)
            kv = ps[:, b, 256 * (h % 2):256 * (h % 2) + 256]
            if c == 0:
                ins = dve.tensor_copy(state[:, h, :], kv)
            else:
                B.wait_full(dve, f"o{c - 1}")
                ins = dve.scalar_tensor_tensor(state[:, h, :], state[:, h, :], dec[:, h, c:c + 1], kv,
                                               ALU.mult, ALU.add)
            if h % 2:
                L.read(ins, B, g)
            else:
                L.done(ins, S("dve_steps"))
        dve.sem_inc(S("state"), 1)
        if c == 0:
            r = K.rstd(0)
            dve_rstd(K, L, B, "conv_var", r)
            L.done(dve.tensor_tensor(conv, conv, wide(r, DT), ALU.mult), S("conv_normed"))
    ga, gb, o = K.tiles(8, DT), K.tiles(9, DT), K.tiles(11, DT)

    def gate_conv(m):
        b = B.wait_full(dve, f"co{m}")
        L.read(dve.scalar_tensor_tensor(ga[:, m, :], ps[:, b, 0:T], K.v("b_co", m), ga[:, m, :], ALU.add, ALU.mult),
               B, f"co{m}")

    for m in range(4):
        gate_conv(m)
    for h in range(GH):
        dve_rstd(K, L, B, f"o_ms{h}", K.rstd(h))
        for m in (2 * h, 2 * h + 1):
            L.done(dve.scalar_tensor_tensor(o[:, m, :], o[:, m, :], K.v("gla_g", m), K.rstd(h), ALU.mult, ALU.mult),
                   S("dve_steps"))
    L.done(dve.tensor_tensor(K.A(7), K.A(7), K.A(11), ALU.mult), S("gla_in"))
    for m in range(4, DT):
        gate_conv(m)
    for m in range(DT):
        b = B.wait_full(dve, f"go{m}")
        L.read(dve.tensor_tensor(gb[:, m, :], ps[:, b, 0:T], gb[:, m, :], ALU.mult), B, f"go{m}")
        L.done(dve.tensor_tensor(ga[:, m, :], ga[:, m, :], gb[:, m, :], ALU.add), S("merged1"))
    x, h1 = K.tiles(0, DT), K.tiles(1, DT)
    for m in range(DT):
        B.wait_read(dve, f"wo{m}")
        L.done(dve.scalar_tensor_tensor(h1[:, m, :], x[:, m, :], ALPHA1, h1[:, m, :], ALU.mult, ALU.add), S("pre_ln1"))
    dve_centre(K, L, B, "ln1_mean", h1, "ln1_centred")
    dve_rstd(K, L, B, "ln1_var", K.rstd(0))
    for m in range(DT):
        L.done(dve.tensor_tensor(h1[:, m, :], h1[:, m, :], K.rstd(0), ALU.mult), S("ln1_scaled"))


def block1_sp(K, sp):
    S, R, d = K.sem, K.ring1, K.d
    by_tile = lambda w: w.rearrange("(k p) n -> p k n", p=P)
    sp.dma_start(K.tiles(0, DT), by_tile(d["x"])).then_inc(S("x_in"), 16)
    w_in = by_tile(d["w_in"])

    def load(slab):
        if slab in IN_COLS:
            src = w_in[:, :, IN_COLS[slab]:IN_COLS[slab] + 512]
        else:
            w = dict(co="w_conv_out", go="w_gla_out", wo="w_out")[slab[:2]]
            src = by_tile(d[w])[:, :, 512 * int(slab[2]):512 * int(slab[2]) + 512]
        R.load(sp, K.banks1, slab, K.slab(R.slot(slab)), src)

    for m in range(4):
        sp.dma_start(K.slab(0)[:, :, m * P:(m + 1) * P], w_in[:, :, O_A + m * P:O_A + (m + 1) * P])\
          .then_inc(S(f"first_in{m}"), 16)
    load("g0")
    sp.dma_start(K.wf[:, :].rearrange("p (k r) -> p k r", k=DT), w_in[:, :, O_F:O_F + RANK]).then_inc(S("params_in"), 16)
    for slab in SLABS1[2:]:
        load(slab)


def load_params(K, eng):
    S, d = K.sem, K.d
    eng.dma_start(K.vec[:, :], d["vecs"]).then_inc(S("params_in"), 16)
    eng.dma_start(K.con[:, :], d["consts"]).then_inc(S("params_in"), 16)
    eng.dma_start(K.rowbuf[32:33, 0:NROW], d["rows"]).then_inc(S("params_in"), 16)
    eng.dma_start(K.w_gate_up(), d["w_gate_up"]).then_inc(S("params_in"), 16)




SETS = [("w1", 0), ("w1", 1), ("w3", 0), ("w3", 1), ("w2", 0), ("w2", 1)]
RSETS = 3
MOE_BANK = dict(pick=(0, 1), turn_sel=2, up=(3, 4), turn_h=5, down=(6, 7), put=(0, 1, 3, 4))


def moe_views(K):
    class V:
        x = K.tiles(0, DT)
        x_rows = K.tiles(1, TT, D)
        total = K.tiles(2, DT)
        picked = K.tiles(3, DT, P)
        sel = K.tiles(3, TT, P, 1024)
        wsel = K.tiles(3, TT, P, 1280)
        wsel_t = K.A(3, T, 1536)
        hidden = K.A(4, DE)
        hidden_t = K.tiles(4, ET, P, DE)
        y = K.A(4, D, 1024)
        w_router = K.tiles(5, DT, NG + NE)
        place = K.tiles(5, TT, NE, 576)
        weight = K.tiles(5, TT, NE, 704)
        chosen = K.tiles(5, TT, NE, 832)
    return V


def moe_set(K, i, k):
    at = (len(SLABS1) + 2 * (i % RSETS)) % RING * SLOT_COLS
    return K.ring_cols(at, 2 * SLOT_COLS).rearrange("p (e k n) -> p e k n", e=QUAD, k=k)


def moe_pe(K, pe):
    S, ps, B = K.sem, K.psum, K.banks1
    V = moe_views(K)
    pe.wait_ge(S("router_in"), 16)
    pe.wait_ge(S("x1"), DT)
    for t in range(TT):
        pe_group(K, pe, B, f"logits{t}", [V.x[:, k, t * P:(t + 1) * P] for k in range(DT)],
                 [V.w_router[:, k, :] for k in range(DT)], out=(slice(0, P), slice(0, NG + NE)), bias=K.row("b_rt"))
    for t in range(TT):
        for half in range(2):
            b = B.take(pe, f"turn_x{t}_{half}")
            for j in range(4):
                m = pe.transpose(ps[:, b, j * P:(j + 1) * P], V.x[:, 4 * half + j, t * P:(t + 1) * P], K.c("ident"))
            m.then_inc(B.full[b], 1)
    pe.wait_ge(S("chosen"), 1)
    pe_group(K, pe, B, "before0", [K.c("before")], [V.chosen[:, 0, :]], out=(slice(0, P), slice(0, NE)))
    pe_group(K, pe, B, "before1", [K.c("ones"), K.c("before")], [V.chosen[:, 0, :], V.chosen[:, 1, :]],
             out=(slice(0, P), slice(0, NE)))
    pe_group(K, pe, B, "chose", [K.c("ones"), K.c("ones")], [V.chosen[:, 0, :], V.chosen[:, 1, :]],
             out=(slice(0, P), slice(0, NE)))
    pe.wait_ge(S("mem_squares"), 1)
    pe_group(K, pe, B, "mem_ms", [K.c("j1024")] * DT, [K.tiles(7, DT)[:, j, :] for j in range(DT)])
    pe.wait_ge(S("rounds_known"), 1)
    rounds = pe.value_load(K.rounds_int[0:1, 0:1], min_val=1, max_val=ROUNDS)
    with pe.Fori(0, rounds) as r:
        with pe.Fori(0, NQ) as q:
            n = r * NQ + q
            pe.wait_ge(S("sel_built"), n * 4 + 4)
            bank = MOE_BANK["turn_sel"]
            for t in range(TT):
                m = pe.transpose(ps[:, bank, t * P:(t + 1) * P], V.wsel[:, t, :], K.c("ident"))
            m.then_inc(S("sel_turned"), 1)
            pe.wait_ge(S("total_added"), n * 4 + 1)
            for half in range(2):
                bank = MOE_BANK["pick"][half]
                for j in range(4):
                    k = 4 * half + j
                    for t in range(TT):
                        m = pe.matmul(ps[:, bank, j * P:(j + 1) * P], V.x_rows[:, t, k::DT],
                                      V.sel[:, t, :], start=(t == 0), stop=(t == TT - 1))
                m.then_inc(S("picked"), 1)
            pe.wait_ge(S("picked_dve"), n + 1)
            pe.wait_ge(S("picked_act"), n + 1)
            for w, bank in enumerate(MOE_BANK["up"]):
                for half in range(2):
                    i = 2 * w + half
                    pe.wait_ge(S(f"moe_landed{i % RSETS}"), n * 32 + 16 * (i // RSETS + 1))
                    part = moe_set(K, i, DT // 2)
                    for j in range(DT // 2):
                        k = DT // 2 * half + j
                        for e in range(QUAD):
                            slots = slice(e * SLOTS, (e + 1) * SLOTS)
                            m = pe.matmul(ps[slots, bank, :], V.picked[:, k, slots], part[:, e, j, :],
                                          start=(k == 0), stop=(k == DT - 1))
                    m.then_inc(S(f"moe_read{i % RSETS}"), 1)
            pe.wait_ge(S("gated"), n + 1)
            for f in range(ET):
                m = pe.transpose(ps[:, MOE_BANK["turn_h"], f * P:(f + 1) * P], V.hidden[:, f::ET],
                                 K.c("ident"))
            m.then_inc(S("h_turned"), 1)
            pe.wait_ge(S("h_saved"), n + 1)
            for half in range(2):
                i = 4 + half
                pe.wait_ge(S(f"moe_landed{i % RSETS}"), n * 32 + 16 * (i // RSETS + 1))
                part = moe_set(K, i, ET // 2)
                for j in range(ET // 2):
                    f = ET // 2 * half + j
                    for c, bank in enumerate(MOE_BANK["down"]):
                        for e in range(QUAD):
                            slots = slice(e * SLOTS, (e + 1) * SLOTS)
                            m = pe.matmul(ps[slots, bank, :], V.hidden_t[:, f, slots],
                                          part[:, e, j, c * 512:(c + 1) * 512], start=(f == 0), stop=(f == ET - 1))
                m.then_inc(S(f"moe_read{i % RSETS}"), 1)
            pe.wait_ge(S("sel_saved"), n + 1)
            pe.wait_ge(S("y_dve"), n + 1)
            pe.wait_ge(S("y_act"), n + 1)
            for j, bank in enumerate(MOE_BANK["put"]):
                for half in range(2):
                    k = 2 * j + half
                    m = pe.matmul(ps[:, bank, half * T:(half + 1) * T], V.y[:, k * P:(k + 1) * P], V.wsel_t,
                                  start=True, stop=True)
                m.then_inc(S("put"), 1)
    pe.drain().then_inc(S("moe_over"), 1)
    x, sq = K.tiles(1, DT), K.tiles(3, DT)
    pe_mean_by_tile(K, pe, B, "ln2_mean", x, "pre_ln2")
    pe_mean_by_tile(K, pe, B, "ln2_var", sq, "ln2_squares")


def moe_act(K, act):
    S, ps, B, L = K.sem, K.psum, K.banks1, K.line("act", act)
    V = moe_views(K)
    W = router_views(K)
    for t in range(TT):
        b = B.wait_full(act, f"logits{t}")
        L.read(act.activation(W.logits[:, t, :], ps[:, b, 0:NG + NE], ACT.Copy), B, f"logits{t}")
    for t in range(TT):
        for half in range(2):
            g = f"turn_x{t}_{half}"
            b = B.wait_full(act, g)
            L.read(act.activation(V.x_rows[:, t, 512 * half:512 * half + 512], ps[:, b, :], ACT.Copy), B, g)
    act.wait_ge(S("group_below"), 1)
    L.done(act.activation(W.gexp, W.gexp, ACT.Exp), S("group_exp"))
    act.wait_ge(S("second_below"), 1)
    L.done(act.activation(W.e2, W.e2, ACT.Exp), S("second_exp"))
    act.wait_ge(S("second_in"), 32)
    L.done(act.activation(K.A(7), K.A(10), ACT.Square), S("mem_squares"))
    act_std(K, L, B, "mem_ms", K.A(8, T), "rms_eps")
    for m in range(DT):
        mem = K.tiles(10, DT)[:, m, :]
        L.done(act.activation(mem, mem, ACT.Copy, scale=K.v("n_mem", m)), S("mem_scaled"))
    act.wait_ge(S("rounds_known"), 1)
    rounds = act.value_load(K.rounds_int[0:1, 0:1], min_val=1, max_val=ROUNDS)
    with act.Fori(0, rounds) as r:
        with act.Fori(0, NQ) as q:
            n = r * NQ + q
            act.wait_ge(S("sel_turned"), n + 1)
            act.activation(V.wsel_t, ps[:, MOE_BANK["turn_sel"], 0:T], ACT.Copy).then_inc(S("sel_saved"), 1)
            act.wait_ge(S("picked"), n * 2 + 2)
            act.activation(K.A(3, 512, 512), ps[:, MOE_BANK["pick"][1], :], ACT.Copy).then_inc(S("picked_act"), 1)
            act.wait_ge(S("moe_read1"), n * 2 + 2)
            act.activation(V.hidden, ps[:, MOE_BANK["up"][0], :], ACT.Silu).then_inc(S("silu"), 1)
            act.wait_ge(S("h_turned"), n + 1)
            act.activation(K.A(4, DE, DE), ps[:, MOE_BANK["turn_h"], :], ACT.Copy).then_inc(S("h_saved"), 1)
            act.wait_ge(S("moe_read2"), n * 2 + 3)
            act.activation(K.A(4, 512, 1536), ps[:, MOE_BANK["down"][1], :], ACT.Copy).then_inc(S("y_act"), 1)
    h2 = K.tiles(1, DT)
    act_squares(K, L, K.tiles(3, DT), h2, "ln2_centred", "ln2_squares")
    act_std(K, L, B, "ln2_var", K.A(4, T), "ln_eps")
    act_affine(K, L, K.tiles(0, DT), h2, "ln2_g", "ln2_b", "ln2_scaled", "x2")


def router_views(K):
    class W:
        logits = K.tiles(6, TT, NG + NE)
        gmax = K.A(6, TT, 144)
        gexp = K.tiles(6, TT, NG, 146)
        gsum = K.A(6, TT, 162)
        eq8 = K.tiles(6, TT, NG, 164)
        oh8 = K.tiles(6, TT, NG, 180)
        best = K.A(6, TT, 196)
        masked = K.tiles(6, TT, NE, 198)
        eq = K.tiles(6, TT, NE, 326)
        oh1 = K.tiles(6, TT, NE, 454)
        oh2 = K.tiles(6, TT, NE, 582)
        m1 = K.A(6, TT, 710)
        m2 = K.A(6, TT, 712)
        e2 = K.A(6, TT, 714)
        w1 = K.A(6, TT, 716)
        w2 = K.A(6, TT, 718)
        most = K.A(6, 1, 720)
        over = K.A(6, ROUNDS, 722)
        count = K.A(6, 1, 730)
        chose = K.A(6, NE, 732)
    return W


def last(ap, n):
    p, a = ap.shape
    return ap.unsqueeze(2).to_broadcast([p, a, n])


def moe_dve(K, dve):
    S, ps, B, L = K.sem, K.psum, K.banks1, K.line("dve", dve)
    V, W = moe_views(K), router_views(K)
    step = S("dve_steps")
    tt = lambda out, a, b, op: L.done(dve.tensor_tensor(out, a, b, op), step)
    ts = lambda out, a, s1, s2, op0, op1=None: L.done(
        dve.tensor_scalar(out, a, s1, s2, op0, op1) if op1 is not None else dve.tensor_scalar(out, a, s1, None, op0), step)
    peak = lambda out, a, op=ALU.max: L.done(dve.tensor_reduce(out, a, AX, op), step)

    def first_max(out, values, scratch, rank, n):
        peak(W.best, values)
        tt(scratch, values, last(W.best, n), ALU.is_equal)
        tt(scratch, scratch, wide(rank, TT), ALU.mult)
        peak(W.gsum, scratch)
        tt(out, scratch, last(W.gsum, n), ALU.is_equal)

    for t in range(TT):
        B.wait_read(dve, f"logits{t}")
    glog = W.logits[:, :, 0:NG]
    first_max(W.oh8, glog, W.eq8, K.c("rank8"), NG)
    tt(W.gexp, glog, last(W.best, NG), ALU.subtract)
    dve.sem_inc(S("group_below"), 1)
    ts(W.eq8, W.oh8, -1.0, BIG, ALU.add, ALU.mult)
    for t in range(TT):
        tt(W.masked[:, t, :].rearrange("p (g e) -> p g e", g=NG),
           W.logits[:, t, NG:].rearrange("p (g e) -> p g e", g=NG), last(W.eq8[:, t, :], EPG), ALU.add)
    first_max(W.oh1, W.masked, W.eq, K.c("rank64"), NE)
    L.done(dve.tensor_copy(W.m1, W.best), step)
    L.done(dve.scalar_tensor_tensor(K.A(6, TT * NE, 198), K.A(6, TT * NE, 454), -4.0 * BIG, K.A(6, TT * NE, 198),
                                    ALU.mult, ALU.add), step)
    first_max(W.oh2, W.masked, W.eq, K.c("rank64"), NE)
    tt(W.e2, W.best, W.m1, ALU.subtract)
    dve.sem_inc(S("second_below"), 1)
    tt(V.chosen, W.oh1, W.oh2, ALU.add)
    dve.sem_inc(S("chosen"), 1)
    dve.wait_ge(S("group_exp"), 1)
    peak(W.gsum, W.gexp, ALU.add)
    L.done(dve.reciprocal(W.gsum, W.gsum), step)
    dve.wait_ge(S("second_exp"), 1)
    ts(W.w1, W.e2, 1.0, None, ALU.add)
    L.done(dve.reciprocal(W.w1, W.w1), step)
    tt(W.w1, W.w1, W.gsum, ALU.mult)
    tt(W.w2, W.w1, W.e2, ALU.mult)
    tt(W.oh1, W.oh1, last(W.w1, NE), ALU.mult)
    tt(W.oh2, W.oh2, last(W.w2, NE), ALU.mult)
    tt(V.weight, W.oh1, W.oh2, ALU.add)
    for t in range(TT):
        b = B.wait_full(dve, f"before{t}")
        L.read(dve.scalar_tensor_tensor(V.place[:, t, :], ps[:, b, 0:NE], 1.0, V.chosen[:, t, :], ALU.add, ALU.mult),
               B, f"before{t}")
    ts(V.place, V.place, -1.0, None, ALU.add)
    b = B.wait_full(dve, "chose")
    L.read(dve.tensor_reduce(W.most, ps[:, b, 0:NE], AX, ALU.max), B, "chose")
    ts(W.over, K.c("rounds"), W.most, None, ALU.is_lt)
    peak(W.count, W.over, ALU.add)
    L.done(dve.tensor_copy(K.rounds_int[:, :], W.count), S("rounds_cast"))
    dve.sem_inc(S("rounds_known"), 1)
    L.done(dve.memset(K.A(2), 0.0), S("total_added"))
    dve_rstd(K, L, B, "mem_ms", K.A(8, T))
    dve.sem_inc(S("mem_rstd"), 1)
    for t in range(TT):
        for half in range(2):
            B.wait_read(dve, f"turn_x{t}_{half}")

    rounds = dve.value_load(K.rounds_int[0:1, 0:1], min_val=1, max_val=ROUNDS)
    by_slot = lambda ap: ap.rearrange("p (e s) -> p e s", e=QUAD)
    with dve.Fori(0, rounds) as r:
        with dve.Fori(0, NQ) as q:
            n = r * NQ + q
            for t in range(TT):
                dve.tensor_tensor(by_slot(V.sel[:, t, :]), wide(K.c("slot_iota"), QUAD),
                                  last(V.place[:, t, bass.ds(q * QUAD, QUAD)], SLOTS), ALU.is_equal)                   .then_inc(S("sel_built"), 1)
            dve.wait_ge(S("sel_built"), n * 4 + 2)
            for t in range(TT):
                dve.tensor_tensor(by_slot(V.wsel[:, t, :]), by_slot(V.sel[:, t, :]),
                                  last(V.weight[:, t, bass.ds(q * QUAD, QUAD)], SLOTS), ALU.mult)                   .then_inc(S("sel_built"), 1)
            dve.wait_ge(S("picked"), n * 2 + 1)
            dve.tensor_copy(K.A(3, 512), ps[:, MOE_BANK["pick"][0], :]).then_inc(S("picked_dve"), 1)
            dve.wait_ge(S("silu"), n + 1)
            dve.wait_ge(S("moe_read0"), n * 2 + 3)
            dve.tensor_tensor(V.hidden, V.hidden, ps[:, MOE_BANK["up"][1], :], ALU.mult).then_inc(S("gated"), 1)
            dve.wait_ge(S("moe_read2"), n * 2 + 3)
            dve.tensor_copy(K.A(4, 512, 1024), ps[:, MOE_BANK["down"][0], :]).then_inc(S("y_dve"), 1)
            for j, bank in enumerate(MOE_BANK["put"]):
                dve.wait_ge(S("put"), n * 4 + j + 1)
                part = K.A(2, 512, 512 * j)
                dve.tensor_tensor(part, part, ps[:, bank, :], ALU.add).then_inc(S("total_added"), 1)
            dve.wait_ge(S("total_added"), n * 4 + 5)
        ins = dve.tensor_scalar(K.A(5, TT * NE, 576), K.A(5, TT * NE, 576), -float(SLOTS), None, ALU.add)
        ins.then_inc(S("round_moved"), 1)
        dve.wait_ge(S("round_moved"), r + 1)
    x1, total, h2 = K.tiles(0, DT), K.tiles(2, DT), K.tiles(1, DT)
    dve.wait_ge(S("x1"), DT)
    for m in range(DT):
        L.done(dve.scalar_tensor_tensor(h2[:, m, :], x1[:, m, :], ALPHA1, total[:, m, :], ALU.mult, ALU.add),
               S("pre_ln2"))
    dve_centre(K, L, B, "ln2_mean", h2, "ln2_centred")
    dve_rstd(K, L, B, "ln2_var", K.A(4, T))
    for m in range(DT):
        L.done(dve.tensor_tensor(h2[:, m, :], h2[:, m, :], K.A(4, T), ALU.mult), S("ln2_scaled"))


def moe_pool(K, pool):
    S = K.sem
    pool.wait_ge(S("mem_scaled"), DT)
    pool.wait_ge(S("mem_rstd"), 1)
    mem = K.tiles(10, DT)
    pool.tensor_tensor(mem, mem, wide(K.A(8, T), DT), ALU.mult).then_inc(S("mem_normed"), 1)


def moe_sp(K, sp):
    S, d = K.sem, K.d
    w = {name: d[name].rearrange("e (p h k) n -> h p e (k n)", p=P, h=2) for name in ("w1", "w3", "w2")}

    def load(i, first, wait):
        name, half = SETS[i]
        sp.wait_ge(S(f"moe_read{i % RSETS}"), wait)
        sp.sem_inc(S("set_wanted"), 1)
        sp.dma_start(moe_set(K, i, 1).rearrange("p e k n -> p e (k n)"), w[name][half, :, bass.ds(first, QUAD), :])\
          .then_inc(S(f"moe_landed{i % RSETS}"), 16)

    for i in range(RSETS):
        load(i, 0, 1)
    sp.wait_ge(S("rounds_known"), 1)
    rounds = sp.value_load(K.rounds_int[0:1, 0:1], min_val=1, max_val=ROUNDS)
    with sp.Fori(0, rounds * NQ - 1) as n:
        for i in range(RSETS, 2 * RSETS):
            load(i, (n & (NQ - 1)) * QUAD, n * 2 + 2)
        for i in range(RSETS):
            load(i, ((n + 1) & (NQ - 1)) * QUAD, n * 2 + 3)
    for i in range(RSETS, 2 * RSETS):
        load(i, (NQ - 1) * QUAD, (rounds * NQ - 1) * 2 + 2)
    sp.wait_ge(S("moe_read0"), rounds * NQ * 2 + 1)
    sp.sem_inc(S("set_wanted"), 1)


GATES = 16
LEVEL_ORDER = [6, 0, 1, 2, 3, 4, 5]


class Views2:
    def __init__(self, K):
        half = lambda s, h: K.tiles(s, HH, T, 1024 * h)
        pair = lambda s, q: K.tiles(s, 2, T, 512 * q)
        self.h, self.u = K.tiles(0, DT), K.tiles(1, DT)
        self.qf, self.key = half(2, 0), half(2, 1)
        self.b, self.logf = half(3, 0), half(3, 1)
        self.decay, self.qd = half(4, 0), half(4, 1)
        self.kd, self.att = half(5, 0), half(5, 1)
        self.prob = [pair(12, i) for i in range(4)]
        self.prob_t = [pair(13, i) for i in range(4)]
        self.hi, self.hg, self.pz, self.sq = (pair(6, i) for i in range(4))
        self.sk = K.A(7, T)
        self.sv = K.tiles(7, TT, ADH, 256)
        self.iq = K.tiles(7, 4, T, 384)
        self.ik = K.A(7, T, 1408)
        self.iw = K.tiles(7, TT, IH, 1664)
        self.rstd = K.A(7, T, 1680)
        self.stat = lambda a, n: K.A(7, n, 1936 + a)
        self.mq, self.mk, self.mv, self.ya = (pair(8, i) for i in range(4))
        self.gate = [K.A(14 + i // DT, T, T * (i % DT)) for i in range(GATES)]
        self.yb, self.yc, self.ym, self.relu1 = (pair(9, i) for i in range(4))
        self.mem = K.tiles(10, DT)
        self.score, self.work, self.not_kept, self.relu2 = (pair(10, i) for i in range(4))
        self.kdec = K.A(10, 1024).rearrange("p (t h k) -> p t h k", t=TT, h=HH)
        self.state = K.A(5, 3 * HH * HDV).rearrange("p (c h v) -> p c h v", c=3, h=HH)
        self.merged = K.rowbuf[:, :].rearrange("p (k t) -> p k t", k=DT)
        self.pool_w = K.wf[:, :].rearrange("p (g d) -> p g d", g=2)



UNITS_UP, UNITS = 2 * FT, 3 * FT
PART_BUFS = 4


class Split:
    def __init__(self, K):
        self.K = K
        whole = lambda s, n, at=0: K.parts(s, n * T, at).rearrange("p (k t) -> p k t", k=n)
        self.u = whole(4, DT), whole(5, DT)
        hid = K.parts(6, 2 * FT * T).rearrange("p (q f t) -> p q f t", q=2, f=FT)
        self.hidden = hid[:, 0], hid[:, 1]
        self.gated = K.arena[:, 2048:2048 + FT * T].rearrange("p (f t) -> p f t", f=FT)

    def part(self, n, low):
        return self.K.parts(12 + n % PART_BUFS, 1024, 1024 * low)

    def source(self, eng, n):
        K, R = self.K, self.K.ring2
        if n < UNITS_UP:
            w = K.slab(R.wait_landed(eng, f"ff{n // 4}"))
            return w[:, :, n % 4 * P:(n % 4 + 1) * P]
        n -= UNITS_UP
        return K.slab(R.wait_landed(eng, f"dn{n // 4}"), 4)[:, n % 4:n % 4 + 1, :]

    def shaped(self, n, low):
        return self.part(n, low).rearrange("p (k n) -> p k n", k=DT if n < UNITS_UP else 1)

    def high(self, L, n):
        K, B, before = self.K, self.K.banks2, n - PART_BUFS
        src = self.source(L.eng, n)
        if before >= UNITS_UP:
            L.eng.wait_ge(K.sem("down_read"), before - UNITS_UP + 1)
        elif before >= 0:
            B.wait_full(L.eng, f"ff{before}")
        L.done(L.eng.activation(self.shaped(n, 0), src, ACT.Copy), K.sem("unit_high"))

    def low(self, L, n):
        K = self.K
        src = self.source(L.eng, n)
        L.eng.wait_ge(K.sem("unit_high"), n + 1)
        L.done(L.eng.tensor_tensor(self.shaped(n, 1), src, self.shaped(n, 0).bitcast(F32), ALU.subtract),
               K.sem("unit_low"))


def three_passes(pe, out, w, x, start, stop):
    pe.matmul(out, w[0], x[0], start=start, stop=False)
    pe.matmul(out, w[0], x[1], start=False, stop=False)
    return pe.matmul(out, w[1], x[0], start=False, stop=stop)


def second_pe(K, pe):
    B, R, S, ps = K.banks2, K.ring2, K.sem, K.psum
    V = Views2(K)
    names = lambda n, a, c: [f"{n}{m}" for m in range(a, a + c)]
    x = V.u

    pe.wait_ge(S("mem_normed"), 1)
    w = K.slab(R.wait_landed(pe, "mem"))
    for m in range(2):
        pe_group(K, pe, B, f"mk{m}", [w[:, k, m * P:(m + 1) * P] for k in range(DT)], [V.mem[:, k, :] for k in range(DT)])
    for t in range(TT):
        pe_group(K, pe, B, f"mv{t}", [V.mem[:, k, t * P:(t + 1) * P] for k in range(DT)],
                 [w[:, k, 256:512] for k in range(DT)])
    R.last_group["mem"] = "mv1"
    pe_mean_by_tile(K, pe, B, "pre_ms", K.tiles(3, DT), "pre_squares")
    w = K.slab(R.wait_landed(pe, "z0"))
    for m in range(4):
        b = B.take(pe, f"hq{m}")
        for k in range(DT):
            if m == 0:
                pe.wait_ge(S("u"), k + 1)
            ins = pe.matmul(ps[:, b, 0:T], w[:, k, m * P:(m + 1) * P], x[:, k, :], start=(k == 0), stop=(k == DT - 1))
        ins.then_inc(B.full[b], 1)
    R.last_group["z0"] = "hq3"
    pe_slab_tiles(K, pe, B, R, "z1", names("hf", 0, 4), x)

    def rows(w, name, c, n):
        for t in range(TT):
            pe_group(K, pe, B, f"{name}{t}", [x[:, k, t * P:(t + 1) * P] for k in range(DT)],
                     [w[:, k, c:c + n] for k in range(DT)], out=(slice(0, P), slice(0, n)))

    def doubled(w, name, c):
        b = B.take(pe, name)
        for half in range(2):
            for k in range(DT):
                m = pe.matmul(ps[64 * half:64 * half + 64, b, 0:T], w[:, k, c:c + 64], x[:, k, :],
                              start=(k == 0), stop=(k == DT - 1))
        m.then_inc(B.full[b], 1)

    def level(i):
        n = LEVEL_ORDER[i]
        pe.wait_ge(S("decayed"), 2 * i + 2)
        q, k = (V.qd, V.kd) if n < LEVELS - 1 else (V.qf, V.key)
        for t in range(TT):
            b = B.take(pe, f"level{n}_{t}")
            for h in range(HH):
                m = pe.matmul(ps[:, b, h * P:(h + 1) * P], k[:, h, t * P:(t + 1) * P], q[:, h, t * P:(t + 1) * P],
                              start=True, stop=True)
            m.then_inc(B.full[b], 1)

    def scores(name, h, q, keys):
        r = slice(64 * (h % 2), 64 * (h % 2) + 64)
        b = B.take(pe, f"{name}{h}")
        for t in range(TT):
            m = pe.matmul(ps[:, b, t * T:(t + 1) * T], q[r, h // 2, t * P:(t + 1) * P], keys(h, r), start=True, stop=True)
        m.then_inc(B.full[b], 1)

    def turn_probs(name, h):
        pe.wait_ge(S(f"{name}_done"), h + 1)
        b = B.take(pe, f"{name}_t{h}")
        for s in range(TT):
            for t in range(TT):
                m = pe.transpose(ps[:, b, (s * TT + t) * P:(s * TT + t + 1) * P],
                                 V.prob[h][:, t, s * P:(s + 1) * P], K.c("ident"))
        m.then_inc(B.full[b], 1)

    def values(name, h, v):
        r = slice(64 * (h % 2), 64 * (h % 2) + 64)
        B.wait_read(pe, f"{name}_t{h}")
        pe_group(K, pe, B, f"{name}_o{h}", [v(h, s) for s in range(TT)], [V.prob_t[h][:, s, :] for s in range(TT)],
                 out=(r, slice(0, T)))

    def gates(i, half):
        pe_slab_tiles(K, pe, B, R, f"gate{i}_{half}", names(f"gate{i}_", 4 * half, 4), x)

    def branch(i, y, slab, place):
        w = K.slab(R.wait_landed(pe, slab), 4)
        for m in range(DT):
            pe_group(K, pe, B, f"br{i}_{m}", [w[:, 2 * place + k, m * P:(m + 1) * P] for k in range(2)],
                     [y[:, k, :] for k in range(2)])
        R.last_group[slab] = f"br{i}_{DT - 1}"

    level(0)
    pe_slab_tiles(K, pe, B, R, "z2", names("hg", 0, 2), x, first=2, last=False)
    rows(K.slab(R.slot("z2")), "hi", 0, 256)
    R.last_group["z2"] = "hi1"
    level(1)
    pe_slab_tiles(K, pe, B, R, "z3", names("pz", 0, 2) + names("sq", 0, 2), x)
    level(2)
    pe_slab_tiles(K, pe, B, R, "z4", names("iq", 0, 3), x, first=1, last=False)
    w = K.slab(R.slot("z4"))
    doubled(w, "sk", 0)
    rows(w, "sv", 64, 64)
    R.last_group["z4"] = "sv1"
    level(3)
    pe_slab_tiles(K, pe, B, R, "z5", ["iq3"], x, last=False)
    w = K.slab(R.slot("z5"))
    doubled(w, "ik", 128)
    rows(w, "iw", 192, 8)
    for m in range(2):
        pe_group(K, pe, B, f"mq{m}", [w[:, k, 200 + m * P:200 + (m + 1) * P] for k in range(DT)],
                 [x[:, k, :] for k in range(DT)])
    R.last_group["z5"] = "mq1"
    level(4)
    gates(1, 0)
    level(5)
    gates(1, 1)
    level(6)
    gates(3, 0)
    pe.wait_ge(S("keys_end"), 1)
    for t in range(TT):
        b = B.take(pe, f"keys_t{t}")
        for h in range(HH):
            m = pe.transpose(ps[:, b, h * P:(h + 1) * P], V.kd[:, h, t * P:(t + 1) * P], K.c("ident"))
        m.then_inc(B.full[b], 1)
    pe.wait_ge(S("pooled"), 4)
    pe.wait_ge(S("pool_w_in"), 16)
    for g in range(4):
        r = slice(64 * (g % 2), 64 * (g % 2) + 64)
        pe_group(K, pe, B, f"pool{g}", [V.pool_w[r, g // 2, :]], [V.pz[r, g // 2, :]], out=(r, slice(0, T)))
    for t in range(TT):
        B.wait_read(pe, f"keys_t{t}")
        B.wait_read(pe, f"hi{t}")
    for c in range(NC - 1):
        t, r = c // 2, slice(CHUNK * (c % 2), CHUNK * (c % 2) + CHUNK)
        b = B.take(pe, f"hkv{c}")
        for h in range(HH):
            m = pe.matmul(ps[:, b, h * HDV:(h + 1) * HDV], V.kdec[r, t, h, :], V.hi[r, t, h * HDV:(h + 1) * HDV],
                          start=True, stop=True)
        m.then_inc(B.full[b], 1)
    for g in ("iq0", "iq1", "iq2", "iq3", "ik"):
        B.wait_read(pe, g)
    for h in range(IH):
        scores("is", h, V.iq, lambda h, r: V.ik[r, :])
    gates(3, 1)
    for g in ("mk0", "mk1", "mq0", "mq1"):
        B.wait_read(pe, g)
    for h in range(AH):
        scores("ms", h, V.mq, lambda h, r: V.mk[r, h // 2, :])
    pe.wait_ge(S("att_done"), 1)
    pe.wait_ge(S("hstate"), NC - 1)
    att = K.A(5, 1024, 1024).rearrange("p (t h s) -> p t h s", t=TT, h=HH)
    for h in range(HH):
        r = slice(64 * (h % 2), 64 * (h % 2) + 64)
        b = B.take(pe, f"ho{h}")
        for t in range(TT):
            pe.matmul(ps[r, b, t * P:(t + 1) * P], V.hi[:, t, h * HDV:(h + 1) * HDV], att[:, t, h, :],
                      start=True, stop=False)
            for c in (2 * t, 2 * t + 1):
                if c:
                    m = pe.matmul(ps[r, b, c * CHUNK:(c + 1) * CHUNK], V.state[:, c - 1, h, :],
                                  V.qd[:, h, c * CHUNK:(c + 1) * CHUNK], start=False, stop=(c % 2 == 1))
        m.then_inc(B.full[b], 1)
    for g in range(4):
        B.wait_read(pe, f"pool{g}")
    branch(1, V.yb, "br13", 0)
    for h in range(AH):
        turn_probs("ms", h)
    for t in range(TT):
        B.wait_read(pe, f"mv{t}")
    for h in range(AH):
        values("ms", h, lambda h, s: V.mv[:, s, h * 64:(h + 1) * 64])
    pe.wait_ge(S("ho_squares"), 1)
    for m in range(2):
        pe_group(K, pe, B, f"ho_ms{m}", [K.c("j64")], [V.relu1[:, m, :]])
    gates(0, 0)
    for h in range(AH):
        B.wait_read(pe, f"ms_o{h}")
    branch(3, V.ym, "br13", 1)
    gates(0, 1)
    for g in ("sq0", "sq1", "sk", "sv0", "sv1"):
        B.wait_read(pe, g)
    for h in range(AH):
        scores("ss", h, V.sq, lambda h, r: V.sk[r, :])
    gates(2, 0)
    pe.wait_ge(S("ya"), 2)
    branch(0, V.ya, "br02", 0)
    for h in range(AH):
        turn_probs("ss", h)
    for h in range(AH):
        values("ss", h, lambda h, s: V.sv[:, s, :])
    gates(2, 1)
    for h in range(AH):
        B.wait_read(pe, f"ss_o{h}")
    branch(2, V.yc, "br02", 1)

    pe.wait_ge(S("merged"), 4 * DT)
    for s in range(2):
        pe_slab_tiles(K, pe, B, R, f"o{s}", names("oz", 4 * s, 4), V.merged)

    pe_mean_by_tile(K, pe, B, "post_ms", K.tiles(3, DT), "post_squares")
    pe_mean_by_tile(K, pe, B, "ffn_ms", K.tiles(3, DT), "ffn_squares")
    sp = Split(K)
    for n in range(UNITS_UP):
        b = B.take(pe, f"ff{n}")
        pe.wait_ge(S("unit_low"), n + 1)
        w = sp.shaped(n, 0), sp.shaped(n, 1)
        for k in range(DT):
            if n == 0:
                pe.wait_ge(S("u_low"), k + 1)
            m = three_passes(pe, ps[:, b, 0:T], [p[:, k, :] for p in w], [p[:, k, :] for p in sp.u], k == 0, k == DT - 1)
        m.then_inc(B.full[b], 1)
    down = []
    for f in range(FT):
        n = UNITS_UP + f
        pe.wait_ge(S("unit_low"), n + 1)
        pe.wait_ge(S("hidden_low"), f + 1)
        for m in range(DT):
            if f == 0:
                down.append(B.take(pe, f"dn{m}"))
            ins = three_passes(pe, ps[:, down[m], 0:T], [sp.part(n, i)[:, m * P:(m + 1) * P] for i in range(2)],
                               [p[:, f, :] for p in sp.hidden], f == 0, f == FT - 1)
            if f == FT - 1:
                ins.then_inc(B.full[down[m]], 1)
            elif m == DT - 1:
                ins.then_inc(S("down_read"), 1)
    pe_mean_by_tile(K, pe, B, "last_ms", K.tiles(3, DT), "last_squares")


def second_act(K, act):
    B, S, ps, L = K.banks2, K.sem, K.psum, K.line("act", act)
    V = Views2(K)

    def evac(group, out, func=ACT.Copy, bias=0.0, scale=1.0, rows=slice(0, P), cols=slice(0, T), sem=None):
        b = B.wait_full(act, group)
        L.read(act.activation(out, ps[rows, b, cols], func, bias=bias, scale=scale), B, group)

    def squares(out, src, sem):
        L.done(act.activation(out, src, ACT.Square), S(sem))

    act_squares(K, L, K.tiles(3, DT), V.h, "x2", "pre_squares")
    for m in range(2):
        evac(f"mk{m}", V.mk[:, m, :])
    for t in range(TT):
        evac(f"mv{t}", V.mv[:, t, :])
    act_std(K, L, B, "pre_ms", V.rstd, "rms_eps")
    act.wait_ge(S("lb_below"), 1)
    L.done(act.activation(V.stat(0, HH), V.stat(0, HH), ACT.Exp), S("lb_exp"))
    for h in range(HH):
        evac(f"hq{h}", V.qf[:, h, :], ACT.Silu)
    for h in range(HH):
        evac(f"hf{h}", V.logf[:, h, :], ACT.Sigmoid)
    act.wait_ge(S("forget"), 1)
    L.done(act.activation(K.A(3, 1024, 1024), K.A(3, 1024, 1024), ACT.Ln), S("log_forget"))

    def level_exp(n):
        act.wait_ge(S("level_below"), n + 1)
        L.done(act.activation(K.A(4, 1024), K.A(4, 1024), ACT.Exp), S("level_exp"))

    level_exp(0)
    for m in range(2):
        evac(f"hg{m}", V.hg[:, m, :], ACT.Silu)
    for t in range(TT):
        evac(f"hi{t}", V.hi[:, t, :])
    level_exp(1)
    for m in range(2):
        evac(f"pz{m}", V.pz[:, m, :])
    for m in range(2):
        evac(f"sq{m}", V.sq[:, m, :], scale=ADH ** -0.5)
    level_exp(2)
    for m in range(3):
        evac(f"iq{m}", V.iq[:, m, :])
    evac("sk", V.sk)
    for t in range(TT):
        evac(f"sv{t}", V.sv[:, t, :], cols=slice(0, ADH))
    level_exp(3)
    evac("iq3", V.iq[:, 3, :])
    evac("ik", V.ik)
    for t in range(TT):
        evac(f"iw{t}", V.iw[:, t, :], scale=IH ** -0.5, cols=slice(0, IH))
    for m in range(2):
        evac(f"mq{m}", V.mq[:, m, :], scale=ADH ** -0.5)

    def exps(name):
        for h in range(AH):
            act.wait_ge(S(f"{name}_below"), h + 1)
            L.done(act.activation(V.prob[h], V.prob[h], ACT.Exp), S(f"{name}_exp"))

    def probs_and_out(name, y):
        for h in range(AH):
            evac(f"{name}_t{h}", V.prob_t[h], cols=slice(0, 512))
        for h in range(AH):
            r = slice(64 * (h % 2), 64 * (h % 2) + 64)
            evac(f"{name}_o{h}", y[r, h // 2, :], rows=r)

    seen = [0]

    def gates(i, half):
        for m in range(4 * half, 4 * half + 4):
            n = seen[0]
            seen[0] += 1
            if n >= GATES:
                act.wait_ge(S("merged"), n - GATES + 1)
            evac(f"gate{i}_{m}", V.gate[n % GATES], ACT.Sigmoid)

    level_exp(4)
    gates(1, 0)
    level_exp(5)
    gates(1, 1)
    act.wait_ge(S("end_below"), 1)
    L.done(act.activation(K.A(4, 1024), K.A(4, 1024), ACT.Exp), S("end_exp"))
    act.wait_ge(S("keys_end"), 1)
    L.done(act.activation(K.A(4, 1024), K.A(3, 1024), ACT.Exp), S("start_exp"))
    gates(3, 0)
    for t in range(TT):
        evac(f"keys_t{t}", K.A(10, 512, 512 * t), cols=slice(0, 512))
    for g in range(4):
        r = slice(64 * (g % 2), 64 * (g % 2) + 64)
        evac(f"pool{g}", V.yb[r, g // 2, :], scale=K.vec[r, VEC["pool_s"][0] + g // 2:VEC["pool_s"][0] + g // 2 + 1],
             rows=r)
    for h in range(IH):
        if h >= 2:
            act.wait_ge(S("indexed"), TT * (h - 1))
        evac(f"is{h}", V.relu1 if h % 2 else V.relu2, ACT.Relu, scale=IDX_SCALE, cols=slice(0, 512))
    gates(3, 1)
    exps("ms")
    for h in range(HH):
        r = slice(64 * (h % 2), 64 * (h % 2) + 64)
        evac(f"ho{h}", V.ya[r, h // 2, :], rows=r)
    squares(K.A(9, 512, 1536), K.A(8, 512, 1536), "ho_squares")
    probs_and_out("ms", V.ym)
    for m in range(2):
        act_std(K, L, B, f"ho_ms{m}", V.relu2[:, m, :], "rms_eps")
    gates(0, 0)
    gates(0, 1)
    exps("ss")
    gates(2, 0)
    probs_and_out("ss", V.yc)
    gates(2, 1)
    sp = Split(K)
    act.wait_ge(S("merged"), 4 * DT)
    for n in range(PART_BUFS):
        sp.high(L, n)
    for m in range(DT):
        evac(f"oz{m}", K.tiles(2, DT)[:, m, :])
        squares(K.tiles(3, DT)[:, m, :], K.tiles(2, DT)[:, m, :], "post_squares")
    act_std(K, L, B, "post_ms", V.rstd, "rms_eps")
    act_squares(K, L, K.tiles(3, DT), V.h, "h2", "ffn_squares")
    act_std(K, L, B, "ffn_ms", V.rstd, "rms_eps")
    for m in range(DT):
        act.wait_ge(S("u2"), m + 1)
        L.done(act.activation(sp.u[0][:, m, :], V.u[:, m, :], ACT.Copy), S("u_high"))
    for n in range(PART_BUFS, UNITS):
        sp.high(L, n)
        g, f = n - PART_BUFS, n - PART_BUFS - FT - 1
        if g < FT:
            evac(f"ff{g}", sp.gated[:, g, :], ACT.Silu)
        if 0 <= f < FT:
            act.wait_ge(S("hidden"), f + 1)
            L.done(act.activation(sp.hidden[0][:, f, :], sp.gated[:, f, :], ACT.Copy), S("hidden_high"))
    for m in range(DT):
        evac(f"dn{m}", V.u[:, m, :])
        squares(K.tiles(3, DT)[:, m, :], V.u[:, m, :], "last_squares")
    act_std(K, L, B, "last_ms", V.rstd, "rms_eps")


IDX_SCALE = 64 ** -0.5


def second_dve(K, dve):
    B, S, ps, L = K.banks2, K.sem, K.psum, K.line("dve", dve)
    V = Views2(K)
    step = S("dve_steps")
    tt = lambda out, a, b, op, sem=step: L.done(dve.tensor_tensor(out, a, b, op), sem)
    ts = lambda out, a, s1, s2, op0, op1, sem=step: L.done(dve.tensor_scalar(out, a, s1, s2, op0, op1), sem)
    stt = lambda out, a, s, b, op0, op1, sem=step: L.done(dve.scalar_tensor_tensor(out, a, s, b, op0, op1), sem)
    peak = lambda out, a, op=ALU.max: L.done(dve.tensor_reduce(out, a, AX, op), step)

    dve.wait_ge(S("second_in"), 32)
    dve.wait_ge(S("x2"), DT)
    dve_rstd(K, L, B, "pre_ms", V.rstd)
    for m in range(DT):
        stt(V.u[:, m, :], V.h[:, m, :], K.v("n_mix_pre", m), V.rstd, ALU.mult, ALU.mult, S("u"))

    lb, keep = V.stat(0, HH), V.stat(HH, HH)
    lbl = K.v("lb", 0, HH)
    tt(lb, lbl, lbl, ALU.max)
    tt(lb, lbl, lb, ALU.subtract)
    dve.sem_inc(S("lb_below"), 1)
    dve.wait_ge(S("lb_exp"), 1)
    L.done(dve.reciprocal(keep, lb), step)
    tt(lb, lb, keep, ALU.mult)
    tt(lb, lb, lb, ALU.subtract)
    ts(keep, lb, -1.0, 1.0, ALU.mult, ALU.add)
    for h in range(HH):
        B.wait_read(dve, f"hf{h}")
        sg = V.logf[:, h, :]
        ts(V.key[:, h, :], sg, -1.0, 1.0, ALU.mult, ALU.add)
        ts(V.key[:, h, :], V.key[:, h, :], keep[:, h:h + 1], None, ALU.mult, ALU.bypass)
        ts(sg, sg, keep[:, h:h + 1], lb[:, h:h + 1], ALU.mult, ALU.add)
    ts(K.A(3, 1024, 1024), K.A(3, 1024, 1024), 1e-30, None, ALU.max, ALU.bypass)
    dve.sem_inc(S("forget"), 1)
    for h in range(HH):
        B.wait_read(dve, f"hq{h}")
    dve.sem_inc(S("decayed"), 2)

    def softmax(name, masked):
        mx = V.stat(8, 2 * AH)
        for h in range(AH):
            b = B.wait_full(dve, f"{name}{h}")
            s = ps[:, b, :].rearrange("p (t k) -> p t k", t=TT)
            m = mx[:, 2 * h:2 * h + 2]
            if masked:
                L.read(dve.tensor_tensor(V.prob[h], s, V.not_kept, ALU.add), B, f"{name}{h}")
                peak(m, V.prob[h])
                tt(V.prob[h], V.prob[h], last(m, T), ALU.subtract)
            else:
                peak(m, s)
                L.read(dve.tensor_tensor(V.prob[h], s, last(m, T), ALU.subtract), B, f"{name}{h}")
            dve.sem_inc(S(f"{name}_below"), 1)
        for h in range(AH):
            m = mx[:, 2 * h:2 * h + 2]
            dve.wait_ge(S(f"{name}_exp"), h + 1)
            peak(m, V.prob[h], ALU.add)
            L.done(dve.reciprocal(m, m), step)
            tt(V.prob[h], V.prob[h], last(m, T), ALU.mult, S(f"{name}_done"))

    count = [0]

    def merge(i):
        for m in range(DT):
            gate = V.gate[count[0] % GATES]
            B.wait_read(dve, f"gate{i}_{m}")
            b = B.wait_full(dve, f"br{i}_{m}")
            out = V.merged[:, m, :] if count[0] < DT else gate
            L.read(dve.tensor_tensor(out, ps[:, b, 0:T], gate, ALU.mult), B, f"br{i}_{m}")
            if count[0] >= DT:
                tt(V.merged[:, m, :], V.merged[:, m, :], gate, ALU.add, S("merged_more"))
            dve.sem_inc(S("merged"), 1)
            count[0] += 1

    def pooling():
        for m in range(2):
            B.wait_read(dve, f"pz{m}")
        z, win, inv = V.pz, [V.relu1, V.yc], K.c2("inv_count").rearrange("p (g t) -> p g t", g=2)
        src = z
        for i, w in enumerate((1, 2, 4, 8)):
            dst = win[i % 2]
            L.done(dve.tensor_copy(dst[:, :, 0:w], src[:, :, 0:w]), step)
            tt(dst[:, :, w:T], src[:, :, w:T], src[:, :, 0:T - w], ALU.add)
            r = slice(64 * (i % 2), 64 * (i % 2) + 64)
            g = i // 2
            out = V.ya[r, g, :]
            tt(out, dst[r, g, :], inv[r, g, :], ALU.mult)
            src = dst
        for g in range(4):
            r = slice(64 * (g % 2), 64 * (g % 2) + 64)
            tt(z[r, g // 2, :], V.ya[r, g // 2, :], z[r, g // 2, :], ALU.subtract, S("pooled"))

    def indexer():
        for t in range(TT):
            B.wait_read(dve, f"iw{t}")
        for h in range(IH):
            B.wait_read(dve, f"is{h}")
            relu = V.relu1 if h % 2 else V.relu2
            for t in range(TT):
                before = K.c2("not_adm").rearrange("p (t k) -> p t k", t=TT) if h == 0 else V.score
                stt(V.score[:, t, :], relu[:, t, :], V.iw[:, t, h:h + 1], before[:, t, :], ALU.mult, ALU.add, S("indexed"))

    def keep_largest():
        top = V.stat(16, 8)
        for t in range(TT):
            for i in range(NSEL // 8):
                src = V.score if i == 0 else V.work
                L.done(dve.max(top, src[:, t, :]), step)
                L.done(dve.match_replace(V.work[:, t, :], top, src[:, t, :], -3e38), step)
        tt(V.not_kept, V.work, V.score, ALU.is_lt)
        flat = lambda i: K.A(10, 512, 512 * i)
        stt(flat(2), flat(0), -0.5 * BIG, flat(2), ALU.is_gt, ALU.mult)
        ts(flat(2), flat(2), -1.0, BIG, ALU.add, ALU.mult)
        dve.sem_inc(S("kept"), 1)

    dve.wait_ge(S("log_forget"), 1)
    L.done(dve.memset(K.A(4, 1024), 1.0), step)
    L.done(dve.memset(K.A(4, 1024).rearrange("p (c s) -> p c s", s=CHUNK)[:, :, 0:1], 0.0), step)
    L.done(dve.tensor_tensor_scan(K.A(3, 1024), K.A(4, 1024), K.A(3, 1024, 1024), 0.0, ALU.mult, ALU.add), step)
    b_all, d_all = K.A(3, 1024), K.A(4, 1024)
    att = K.A(5, 1024, 1024)

    def decay_level(n):
        half = 32 >> n
        v = lambda a: a.rearrange("p (c s) -> p c s", s=2 * half)
        mid = v(b_all)[:, :, half - 1:half].to_broadcast([P, 1024 // (2 * half), 2 * half])
        tt(v(d_all), v(b_all), mid, ALU.subtract)
        stt(d_all, d_all, -1.0, d_all, ALU.mult, ALU.min)
        dve.sem_inc(S("level_below"), 1)
        dve.wait_ge(S("level_exp"), n + 1)
        dve.tensor_tensor(K.A(4, 1024, 1024), K.A(2, 1024), d_all, ALU.mult).then_inc(S("decayed"), 1)
        dve.tensor_tensor(K.A(5, 1024), K.A(2, 1024, 1024), d_all, ALU.mult).then_inc(S("decayed"), 1)
        dve.wait_ge(S("decayed"), 2 * n + 4)

    def add_level(n):
        mask = K.c2("level")[:, n * P:(n + 1) * P]
        for t in range(TT):
            g = f"level{n}_{t}"
            b = B.wait_full(dve, g)
            part = att[:, 512 * t:512 * t + 512]
            out = part if n == LEVEL_ORDER[0] else K.A(10, 512)
            heads = lambda a: a.rearrange("p (h s) -> p h s", h=HH)
            L.read(dve.tensor_tensor(heads(out), heads(ps[:, b, :]), wide(mask, HH), ALU.mult), B, g)
            if n != LEVEL_ORDER[0]:
                tt(part, part, out, ALU.add)

    decay_level(0)
    add_level(LEVELS - 1)
    for n in range(LEVELS - 1):
        add_level(n)
        if n < LEVELS - 2:
            decay_level(n + 1)
    dve.sem_inc(S("att_done"), 1)
    v = lambda a: a.rearrange("p (c s) -> p c s", s=CHUNK)
    end = v(b_all)[:, :, CHUNK - 1:CHUNK]
    tt(v(d_all), end.to_broadcast([P, HH * NC, CHUNK]), v(b_all), ALU.subtract)
    dve.sem_inc(S("end_below"), 1)
    dve.wait_ge(S("end_exp"), 1)
    tt(K.A(5, 1024), K.A(2, 1024, 1024), d_all, ALU.mult)
    dve.sem_inc(S("keys_end"), 1)
    dve.wait_ge(S("start_exp"), 1)
    tt(K.A(4, 1024, 1024), K.A(2, 1024), d_all, ALU.mult)
    pooling()
    whole = d_all.rearrange("p (h c s) -> p h c s", h=HH, c=NC)
    for c in range(NC - 1):
        b = B.wait_full(dve, f"hkv{c}")
        for h in range(HH):
            kv = ps[:, b, h * HDV:(h + 1) * HDV]
            out = V.state[:, c, h, :]
            if c == 0:
                ins = dve.tensor_copy(out, kv)
            else:
                ins = dve.scalar_tensor_tensor(out, V.state[:, c - 1, h, :], whole[:, h, c, CHUNK - 1:CHUNK], kv,
                                               ALU.mult, ALU.add)
            if h == HH - 1:
                L.read(ins, B, f"hkv{c}")
            else:
                L.done(ins, step)
        dve.sem_inc(S("hstate"), 1)
    indexer()
    softmax("ms", False)
    merge(1)
    for m in range(2):
        r = V.relu2[:, m, :]
        dve_rstd(K, L, B, f"ho_ms{m}", r)
        stt(r, r, K.v("hg_g", m), V.hg[:, m, :], ALU.mult, ALU.mult)
        tt(V.ya[:, m, :], V.ya[:, m, :], r, ALU.mult, S("ya"))
    keep_largest()
    merge(3)
    softmax("ss", True)
    merge(0)
    merge(2)

    def add_normed(z, group, gain, sem):
        dve_rstd(K, L, B, group, V.rstd)
        for m in range(DT):
            stt(z[:, m, :], z[:, m, :], K.v(gain, m), V.rstd, ALU.mult, ALU.mult)
            tt(V.h[:, m, :], V.h[:, m, :], z[:, m, :], ALU.add, S(sem))

    sp = Split(K)
    for n in range(PART_BUFS):
        sp.low(L, n)
    add_normed(K.tiles(2, DT), "post_ms", "n_mix_post", "h2")
    dve_rstd(K, L, B, "ffn_ms", V.rstd)

    def u_low(m):
        dve.wait_ge(S("u_high"), m + 1)
        tt(sp.u[1][:, m, :], V.u[:, m, :], sp.u[0][:, m, :].bitcast(F32), ALU.subtract, S("u_low"))

    for m in range(DT):
        stt(V.u[:, m, :], V.h[:, m, :], K.v("n_ffn_pre", m), V.rstd, ALU.mult, ALU.mult, S("u2"))
        if m:
            u_low(m - 1)
    u_low(DT - 1)
    for n in range(PART_BUFS, UNITS):
        sp.low(L, n)
        f = n - PART_BUFS - FT
        if 0 <= f < FT:
            g = f"ff{FT + f}"
            b = B.wait_full(dve, g)
            B.wait_read(dve, f"ff{f}")
            L.read(dve.tensor_tensor(sp.gated[:, f, :], sp.gated[:, f, :], ps[:, b, 0:T], ALU.mult), B, g)
            dve.sem_inc(S("hidden"), 1)
        f -= 1
        if 0 <= f < FT:
            dve.wait_ge(S("hidden_high"), f + 1)
            tt(sp.hidden[1][:, f, :], sp.gated[:, f, :], sp.hidden[0][:, f, :].bitcast(F32), ALU.subtract,
               S("hidden_low"))
    add_normed(V.u, "last_ms", "n_ffn_post", "out")


def second_sp(K, sp):
    S, R, B, d = K.sem, K.ring2, K.banks2, K.d
    by_tile = lambda w: w.rearrange("(k p) n -> p k n", p=P)
    def load(slab, src, k=DT):
        view = K.slab(R.slot(slab), k)
        R.load(sp, B, slab, view[:, 0:src.shape[1], 0:src.shape[2]], src)

    load("mem", by_tile(d["w_mem_kv_2"]))
    for i in range(6):
        load(f"z{i}", by_tile(d["w_in_2"])[:, :, 512 * i:min(512 * i + 512, N_IN2)])
        if i == 0:
            sp.wait_ge(S("moe_over"), 1)
            sp.dma_start(Views2(K).pool_w, d["pool_w_2"].rearrange("(a b) c d -> (b c) a d", b=2)).then_inc(S("pool_w_in"), 16)

    def gates(i, *halves):
        for s in halves or (0, 1):
            load(f"gate{i}_{s}", by_tile(d["w_gate_2"][i])[:, :, 512 * s:512 * s + 512])

    def branches(first):
        src = d["w_branch_2"].rearrange("(a b) (k p) n -> b p a k n", b=2, p=P)[first]
        slab = f"br{first}{first + 2}"
        R.wait_free(sp, B, slab)
        view = K.slab(R.slot(slab), 4)
        for a in range(2):
            sp.dma_start(view[:, 2 * a:2 * a + 2, :], src[:, a]).then_inc(R.landed[R.slot(slab)], 16)

    gates(1)
    gates(3)
    branches(1)
    gates(0)
    gates(2, 0)
    branches(0)
    gates(2, 1)
    for s in range(2):
        load(f"o{s}", by_tile(d["w_out_2"])[:, :, 512 * s:512 * s + 512])

    def load_split(i, slab, src, k):
        slot = R.slot(slab)
        if i < RING2:
            R.wait_free(sp, B, slab)
        else:
            sp.wait_ge(S("unit_low"), 4 * (i - RING2 + 1))
        sp.dma_start(K.slab(slot, k)[:, 0:src.shape[1], :], src).then_inc(R.landed[slot], 16)

    for i in range(11):
        load_split(i, f"ff{i}", by_tile(d["w_ffn_gate_up_2"])[:, :, 512 * i:512 * i + 512], DT)
    for i in range(6):
        load_split(11 + i, f"dn{i}", by_tile(d["w_ffn_down_2"])[:, 4 * i:min(4 * i + 4, FT), :], 4)


def host_arrays(inputs):
    a = {n: np.asarray(v) for n, v in inputs.items()}
    col = lambda v: np.ascontiguousarray(v).reshape(-1, P).T
    b = a["b_in"][0]
    f = np.zeros((P,), np.float32)
    f[:RANK] = b[O_F:O_F + RANK]
    packed = dict(b_a=col(b[O_A:O_A + D]), b_g=col(b[O_G:O_G + D]), b_q=col(b[O_Q:O_Q + GDK]),
                  b_r=col(b[O_R:O_R + D]), b_f=f[:, None], b_ga=col(b[O_GA:O_GA + D]), b_gb=col(b[O_GB:O_GB + D]),
                  conv_w=a["conv_w"][0].reshape(CW, DT, P).transpose(2, 1, 0).reshape(P, DT * CW),
                  conv_b=col(a["conv_b"]), cln_g=col(a["conv_ln_g"]), cln_b=col(a["conv_ln_b"]),
                  b_co=col(a["b_conv_out"]), gla_g=col(a["gla_norm_g"]), b_out=col(a["b_out"]),
                  ln1_g=col(a["ln1_g"]), ln1_b=col(a["ln1_b"]), ln2_g=col(a["ln2_g"]), ln2_b=col(a["ln2_b"]),
                  lb=col(a["lb_logits_2"]), hg_g=col(a["hgrn_norm_2"]), pool_s=col(a["pool_scale_2"]),
                  n_mem=col(a["norm_mem_2"]), n_mix_pre=col(a["norm_mix_pre_2"]),
                  n_mix_post=col(a["norm_mix_post_2"]), n_ffn_pre=col(a["norm_ffn_pre_2"]),
                  n_ffn_post=col(a["norm_ffn_post_2"]))
    assert all(packed[n].shape[1] == m for n, m in VEC_SIZES.items())
    con, con2 = constants()
    out = {
        "x": np.ascontiguousarray(a["x"][0].T), "mem": np.ascontiguousarray(a["mem_2"][0].T),
        "vecs": np.ascontiguousarray(np.concatenate([packed[n] for n in VEC_SIZES], 1)),
        "rows": np.concatenate([b[O_K:O_K + GDK], b[O_V:O_V + GDV],
                                a["b_router_group"][0], a["b_router_expert"][0]])[None, :],
        "w_gate_up": np.concatenate([a["w_gate_up"][0], a["b_gate_up"]], 0),
        "w_router": np.concatenate([a["w_router_group"][0], a["w_router_expert"][0]], 1),
        "consts": con, "consts2": con2,
    }
    for n in ("w_in", "w_conv_out", "w_gla_out", "w_out", "w1", "w3", "w2", "w_in_2", "w_gate_2",
              "w_branch_2", "w_out_2", "pool_w_2", "w_mem_kv_2", "w_ffn_gate_up_2", "w_ffn_down_2"):
        out[n] = a[n][0]
    return {n: np.ascontiguousarray(v) for n, v in out.items()}


INPUTS = ("x", "mem", "vecs", "rows", "consts", "consts2", "w_router", "w_in", "w_conv_out", "w_gate_up", "w_gla_out",
          "w_out", "w1", "w3", "w2", "w_in_2", "w_gate_2", "w_branch_2", "w_out_2", "pool_w_2", "w_mem_kv_2",
          "w_ffn_gate_up_2", "w_ffn_down_2")


def two_blocks(nc, d, out):
    with ExitStack() as ctx:
        K = Chip(nc, ctx, d)
        block = ctx.enter_context(nc.Block())

        @block.tensor
        def _(pe):
            block1_pe(K, pe)
            moe_pe(K, pe)
            second_pe(K, pe)

        @block.scalar
        def _(act):
            load_params(K, act)
            block1_act(K, act)
            moe_act(K, act)
            second_act(K, act)

        @block.vector
        def _(dve):
            block1_dve(K, dve)
            moe_dve(K, dve)
            second_dve(K, dve)

        @block.gpsimd
        def _(pool):
            moe_pool(K, pool)

        @block.sync
        def _(sp):
            block1_sp(K, sp)
            sp.wait_ge(K.sem("o_squares"), 1)
            sp.dma_start(moe_views(K).w_router, d["w_router"].rearrange("(k p) n -> p k n", p=P))\
              .then_inc(K.sem("router_in"), 16)
            sp.wait_ge(K.sem("gla_in"), 1)
            sp.dma_start(K.A(11, NCON2), d["consts2"]).then_inc(K.sem("second_in"), 16)
            sp.dma_start(K.tiles(10, DT), d["mem"].rearrange("(k p) t -> p k t", p=P)).then_inc(K.sem("second_in"), 16)
            moe_sp(K, sp)
            second_sp(K, sp)
            for half in range(2):
                k = slice(DT // 2 * half, DT // 2 * (half + 1))
                sp.wait_ge(K.sem("out"), DT // 2 * (half + 1))
                sp.dma_start(out.rearrange("(k p) t -> p k t", p=P)[:, k, :], K.tiles(0, DT)[:, k, :])\
                  .then_inc(K.sem("stored"), 16)
            sp.wait_ge(K.sem("stored"), 32)


def kernel(**inputs):
    import concourse.bacc as bacc
    from concourse.bass_utils import run_bass_kernel_spmd

    arrays = host_arrays(inputs)
    arrays = {f"in_{n}": arrays[n] for n in INPUTS}
    nc = bacc.Bacc("TRN2", target_bir_lowering=False, num_devices=1)
    d = {n: nc.dram_tensor(f"in_{n}", arrays[f"in_{n}"].shape, F32, kind="ExternalInput").ap() for n in INPUTS}
    out = nc.dram_tensor("out_0", (D, T), F32, kind="ExternalOutput").ap()
    two_blocks(nc, d, out)
    r = run_bass_kernel_spmd(nc, [arrays], core_ids=[0])
    return np.ascontiguousarray(r.results[0]["out_0"].T)[None]
```
